# Optimizing a Trainium2 kernel written in Bass

```python
import jax, jax.numpy as jnp
from jax import lax
import numpy as np

D_MODEL = 1024
BATCH = 1
SEQ = 512
DEPTH = 1

CHUNK = 64
N_META = 16
Q_BLOCK = 128
EPS = 1e-6
GLA_HEADS = 4
GLA_DK = 64
GLA_DV = 128
GLA_GATE_RANK = 16
GLA_TAU = 16.0
GLA_QK = GLA_HEADS * GLA_DK
GLA_VW = GLA_HEADS * GLA_DV
MLA_HEADS = 4
MLA_Q_RANK = 256
MLA_KV_RANK = 128
MLA_NOPE = 128
MLA_ROPE = 64
MLA_V = 128
MLA_OUT = MLA_HEADS * MLA_V
ROPE_BASE = 10000.0
D_MIX = GLA_VW + MLA_OUT
IN_WIDTHS = (GLA_QK, GLA_QK, GLA_VW, GLA_VW, GLA_GATE_RANK, MLA_Q_RANK, MLA_KV_RANK, MLA_ROPE)
D_IN = sum(IN_WIDTHS)
N_GROUPS = 8
EXPERTS_PER_GROUP = 8
N_EXPERTS = N_GROUPS * EXPERTS_PER_GROUP
TOP_K = 2
D_EXPERT = 512
MOE_BLOCK = 128


def rmsnorm(x, gain):
    x32 = x.astype(jnp.float32)
    y = x32 * lax.rsqrt(jnp.mean(x32 * x32, axis=-1, keepdims=True) + EPS)
    return (y * gain.astype(jnp.float32)).astype(x.dtype)

def split_points():
    pts, acc = [], 0
    for w in IN_WIDTHS[:-1]:
        acc += w
        pts.append(acc)
    return pts

def chunk_ids(length):
    p = jnp.arange(length)
    return jnp.where(p < N_META, 0, 1 + (p - N_META) // CHUNK)

def rope_tables(length):
    pos = jnp.arange(length, dtype=jnp.float32)
    inv = ROPE_BASE ** (-jnp.arange(0, MLA_ROPE, 2, dtype=jnp.float32) / MLA_ROPE)
    ang = pos[:, None] * inv[None, :]
    return jnp.cos(ang), jnp.sin(ang)

def apply_rope(x, cos, sin):
    half = x.shape[-1] // 2
    x1, x2 = x[..., :half].astype(jnp.float32), x[..., half:].astype(jnp.float32)
    return jnp.concatenate([x1 * cos - x2 * sin, x2 * cos + x1 * sin], axis=-1).astype(x.dtype)

def gla_group(q, k, v, r, a_low, w_a2, b_a, out_gain):
    f32 = jnp.float32
    B, L, _ = q.shape
    pad = (-L) % CHUNK
    log_a = jax.nn.log_sigmoid((a_low @ w_a2 + b_a).astype(f32)) / GLA_TAU

    def prep(t, d):
        t = jnp.pad(t.astype(f32), ((0, 0), (pad, 0), (0, 0)))
        n = t.shape[1] // CHUNK
        return t.reshape(B, n, CHUNK, GLA_HEADS, d).transpose(0, 3, 1, 2, 4)

    qc = prep(q, GLA_DK) * (GLA_DK ** -0.5)
    kc = prep(k, GLA_DK)
    vc = prep(v, GLA_DV)
    b = jnp.cumsum(prep(log_a, GLA_DK), axis=3)
    b_last = b[:, :, :, -1:, :]
    q_e = qc * jnp.exp(b)
    causal = jnp.tril(jnp.ones((CHUNK, CHUNK), dtype=bool))
    att = jnp.where(causal, jnp.einsum('bhncd,bhnsd->bhncs', q_e, kc * jnp.exp(-b)), 0.0)
    o = jnp.einsum('bhncs,bhnse->bhnce', att, vc)
    upd = jnp.einsum('bhncd,bhnce->nbhde', kc * jnp.exp(b_last - b), vc)
    decay = jnp.exp(b_last[:, :, :, 0, :]).transpose(2, 0, 1, 3)

    def step(s, inp):
        dec, u = inp
        return dec[..., None] * s + u, s

    s0 = jnp.zeros((B, GLA_HEADS, GLA_DK, GLA_DV), f32)
    _, s_prev = lax.scan(step, s0, (decay, upd))
    o = o + jnp.einsum('bhncd,nbhde->bhnce', q_e, s_prev)
    o = o.transpose(0, 2, 3, 1, 4).reshape(B, -1, GLA_HEADS, GLA_DV)[:, pad:]
    o = o * lax.rsqrt(jnp.mean(o * o, axis=-1, keepdims=True) + EPS)
    o = o.reshape(B, L, GLA_VW) * out_gain.astype(f32)
    return (o * jax.nn.silu(r.astype(f32))).astype(q.dtype)

def mla_group(q_lat, kv_lat, k_rope, q_norm, w_qb, kv_norm, w_kvb):
    B, L, _ = q_lat.shape
    q = (rmsnorm(q_lat, q_norm) @ w_qb).reshape(B, L, MLA_HEADS, MLA_NOPE + MLA_ROPE)
    q_nope, q_rope = q[..., :MLA_NOPE], q[..., MLA_NOPE:]
    kv = (rmsnorm(kv_lat, kv_norm) @ w_kvb).reshape(B, L, MLA_HEADS, MLA_NOPE + MLA_V)
    k_nope, v = kv[..., :MLA_NOPE], kv[..., MLA_NOPE:]
    cos, sin = rope_tables(L)
    q_rope = apply_rope(q_rope, cos[:, None, :], sin[:, None, :])
    k_rope = apply_rope(k_rope, cos, sin)
    key_chunk = chunk_ids(L)
    scale = (MLA_NOPE + MLA_ROPE) ** -0.5

    def attend(args):
        qn, qr, qcid = args
        s = (jnp.einsum('bqhd,bkhd->bhqk', qn, k_nope)
             + jnp.einsum('bqhd,bkd->bhqk', qr, k_rope)).astype(jnp.float32) * scale
        s = jnp.where(key_chunk[None, None, None, :] <= qcid[None, None, :, None], s, -jnp.inf)
        p = jax.nn.softmax(s, axis=-1).astype(v.dtype)
        return jnp.einsum('bhqk,bkhd->bqhd', p, v)

    meta_out = attend((q_nope[:, :N_META], q_rope[:, :N_META], key_chunk[:N_META]))
    nb = (L - N_META) // Q_BLOCK

    def blocks(t):
        return t[:, N_META:].reshape(B, nb, Q_BLOCK, *t.shape[2:]).swapaxes(0, 1)

    blk = lax.map(attend, (blocks(q_nope), blocks(q_rope), key_chunk[N_META:].reshape(nb, Q_BLOCK)))
    blk = blk.swapaxes(0, 1).reshape(B, L - N_META, MLA_HEADS, MLA_V)
    return jnp.concatenate([meta_out, blk], axis=1).reshape(B, L, MLA_OUT)

def hier_moe(u, wg, bg, we, be, w_gate, w_up, w_down):
    f32 = jnp.float32
    B, L, D = u.shape
    t = u.reshape(-1, D)
    n_tok = t.shape[0]
    g_prob = jax.nn.softmax((t @ wg + bg).astype(f32), axis=-1)
    g_p, g_idx = lax.top_k(g_prob, 1)
    e_logits = (t @ we + be).astype(f32).reshape(n_tok, N_GROUPS, EXPERTS_PER_GROUP)
    e_logits = jnp.take_along_axis(e_logits, g_idx[:, :, None], axis=1)[:, 0]
    e_p, e_idx = lax.top_k(jax.nn.softmax(e_logits, axis=-1), TOP_K)
    gates = g_p * e_p / jnp.sum(e_p, axis=-1, keepdims=True)
    expert = g_idx * EXPERTS_PER_GROUP + e_idx
    e_flat = expert.reshape(-1)
    tok_flat = jnp.repeat(jnp.arange(n_tok, dtype=jnp.int32), TOP_K)
    gate_flat = gates.reshape(-1)
    order = jnp.argsort(e_flat)
    e_sorted, tok_sorted, gate_sorted = e_flat[order], tok_flat[order], gate_flat[order]
    counts = jnp.bincount(e_flat, length=N_EXPERTS)
    padded = (counts + MOE_BLOCK - 1) // MOE_BLOCK * MOE_BLOCK
    pad_end = jnp.cumsum(padded)
    pad_start = pad_end - padded
    seg_start = jnp.cumsum(counts) - counts
    n_assign = n_tok * TOP_K
    dest = pad_start[e_sorted] + jnp.arange(n_assign) - seg_start[e_sorted]
    n_blocks = -(-(n_assign + N_EXPERTS * (MOE_BLOCK - 1)) // MOE_BLOCK)
    n_slots = n_blocks * MOE_BLOCK
    slot_tok = jnp.full((n_slots,), n_tok, jnp.int32).at[dest].set(tok_sorted)
    slot_gate = jnp.zeros((n_slots,), f32).at[dest].set(gate_sorted)
    block_expert = jnp.minimum(
        jnp.searchsorted(pad_end, jnp.arange(n_blocks) * MOE_BLOCK, side='right'), N_EXPERTS - 1)
    t_pad = jnp.concatenate([t, jnp.zeros((1, D), t.dtype)], axis=0)
    xs = t_pad[slot_tok].reshape(n_blocks, MOE_BLOCK, D)

    def expert_block(args):
        xb, e = args
        hdn = jax.nn.silu(xb @ w_gate[e]) * (xb @ w_up[e])
        return hdn @ w_down[e]

    ys = lax.map(expert_block, (xs, block_expert)).reshape(n_slots, D)
    out = jnp.zeros((n_tok + 1, D), f32).at[slot_tok].add(ys.astype(f32) * slot_gate[:, None])[:n_tok]
    return out.reshape(B, L, D).astype(u.dtype)

def first_inputs(seed: int = 0) -> dict:
    key = jax.random.key(seed)
    ks = jax.random.split(key, 24)
    f32 = jnp.float32

    def nrm(k, shape, scale):
        return jax.random.normal(k, shape, f32) * scale

    def gain(k, shape):
        return 1.0 + 0.02 * jax.random.normal(k, shape, f32)

    return {
        'x': nrm(ks[0], (BATCH, SEQ, D_MODEL), 1.0),
        'meta_tokens': nrm(ks[1], (N_META, D_MODEL), 1.0),
        'mix_norm': gain(ks[2], (DEPTH, D_MODEL)),
        'w_in': nrm(ks[3], (DEPTH, D_MODEL, D_IN), D_MODEL ** -0.5),
        'gla_w_a2': nrm(ks[4], (DEPTH, GLA_GATE_RANK, GLA_QK), GLA_GATE_RANK ** -0.5),
        'gla_b_a': nrm(ks[5], (DEPTH, GLA_QK), 0.1),
        'gla_out_norm': gain(ks[6], (DEPTH, GLA_VW)),
        'mla_q_norm': gain(ks[7], (DEPTH, MLA_Q_RANK)),
        'mla_w_qb': nrm(ks[8], (DEPTH, MLA_Q_RANK, MLA_HEADS * (MLA_NOPE + MLA_ROPE)), MLA_Q_RANK ** -0.5),
        'mla_kv_norm': gain(ks[9], (DEPTH, MLA_KV_RANK)),
        'mla_w_kvb': nrm(ks[10], (DEPTH, MLA_KV_RANK, MLA_HEADS * (MLA_NOPE + MLA_V)), MLA_KV_RANK ** -0.5),
        'w_out': nrm(ks[11], (DEPTH, D_MIX, D_MODEL), D_MIX ** -0.5),
        'ffn_norm': gain(ks[12], (DEPTH, D_MODEL)),
        'router_group_w': nrm(ks[13], (DEPTH, D_MODEL, N_GROUPS), D_MODEL ** -0.5),
        'router_group_b': nrm(ks[14], (DEPTH, N_GROUPS), 0.01),
        'router_expert_w': nrm(ks[15], (DEPTH, D_MODEL, N_EXPERTS), D_MODEL ** -0.5),
        'router_expert_b': nrm(ks[16], (DEPTH, N_EXPERTS), 0.01),
        'expert_w_gate': nrm(ks[17], (DEPTH, N_EXPERTS, D_MODEL, D_EXPERT), D_MODEL ** -0.5),
        'expert_w_up': nrm(ks[18], (DEPTH, N_EXPERTS, D_MODEL, D_EXPERT), D_MODEL ** -0.5),
        'expert_w_down': nrm(ks[19], (DEPTH, N_EXPERTS, D_EXPERT, D_MODEL), D_EXPERT ** -0.5),
        'final_norm': gain(ks[20], (D_MODEL,)),
    }

def first_block(x, meta_tokens, mix_norm, w_in, gla_w_a2, gla_b_a, gla_out_norm, mla_q_norm, mla_w_qb,
              mla_kv_norm, mla_w_kvb, w_out, ffn_norm, router_group_w, router_group_b, router_expert_w,
              router_expert_b, expert_w_gate, expert_w_up, expert_w_down, final_norm):
    B = x.shape[0]
    meta = jnp.broadcast_to(meta_tokens[None].astype(x.dtype), (B, N_META, x.shape[-1]))
    h = jnp.concatenate([meta, x], axis=1)
    pts = split_points()
    for l in range(DEPTH):
        u = rmsnorm(h, mix_norm[l])
        z = u @ w_in[l]
        q, k, v, r, a_low, q_lat, kv_lat, k_rope = jnp.split(z, pts, axis=-1)
        y_gla = gla_group(q, k, v, r, a_low, gla_w_a2[l], gla_b_a[l], gla_out_norm[l])
        y_mla = mla_group(q_lat, kv_lat, k_rope, mla_q_norm[l], mla_w_qb[l], mla_kv_norm[l], mla_w_kvb[l])
        h = h + jnp.concatenate([y_gla, y_mla], axis=-1) @ w_out[l]
        h = h + hier_moe(rmsnorm(h, ffn_norm[l]), router_group_w[l], router_group_b[l], router_expert_w[l],
                         router_expert_b[l], expert_w_gate[l], expert_w_up[l], expert_w_down[l])
    return rmsnorm(h, final_norm)[:, N_META:]


HG_HEADS = 8
HG_DK = 64
HG_DV = 64
HG_WIDTH = HG_HEADS * HG_DK
CONV_WIDTH = 512
CONV_K = 3
N_BRANCH = 2
PEER_HEADS = 8
PEER_NKEYS = 128
PEER_N = PEER_NKEYS * PEER_NKEYS
PEER_QDIM = 256
PEER_HALF = PEER_QDIM // 2
PEER_TOPK = 16
PEER_BLOCK = 128
IN_SPLITS = [HG_WIDTH] * 4 + [CONV_WIDTH] * 3 + [N_BRANCH * D_MODEL]
IN_COLS = sum(IN_SPLITS)


def rmsnorm_2(x, g):
    xf = x.astype(jnp.float32)
    y = xf * lax.rsqrt(jnp.mean(xf * xf, axis=-1, keepdims=True) + EPS)
    return (y * g.astype(jnp.float32)).astype(x.dtype)

def hgrn2_chunkwise(q, k, log_f, v):
    b_, s_, h_, dk = q.shape
    dv = v.shape[-1]
    nc = s_ // CHUNK

    def to_chunks(t):
        return t.astype(jnp.float32).reshape(b_, nc, CHUNK, h_, t.shape[-1]).transpose(1, 0, 3, 2, 4)

    qc, kc, fc, vc = to_chunks(q), to_chunks(k), to_chunks(log_f), to_chunks(v)
    causal = jnp.tril(jnp.ones((CHUNK, CHUNK), dtype=bool))

    def step(state, inp):
        q_, k_, lf, v_ = inp
        b = jnp.cumsum(lf, axis=-2)
        b_last = b[..., -1:, :]
        o_inter = jnp.einsum('bhtd,bhde->bhte', q_ * jnp.exp(b), state)
        rel = jnp.where(causal[:, :, None], b[..., :, None, :] - b[..., None, :, :], -jnp.inf)
        scores = jnp.einsum('bhtd,bhsd,bhtsd->bhts', q_, k_, jnp.exp(rel))
        o = o_inter + jnp.einsum('bhts,bhse->bhte', scores, v_)
        new_state = (jnp.exp(b_last[..., 0, :])[..., None] * state
                     + jnp.einsum('bhsd,bhse->bhde', k_ * jnp.exp(b_last - b), v_))
        return new_state, o

    s0 = jnp.zeros((b_, h_, dk, dv), jnp.float32)
    _, o = lax.scan(step, s0, (qc, kc, fc, vc))
    return o.transpose(1, 0, 3, 2, 4).reshape(b_, s_, h_, dv)

def causal_depthwise_conv(u, w):
    c = u.shape[-1]
    return lax.conv_general_dilated(
        u, w[:, None, :].astype(u.dtype), window_strides=(1,), padding=[(CONV_K - 1, 0)],
        dimension_numbers=('NWC', 'WIO', 'NWC'), feature_group_count=c)

def peer_ffn(h, w_query, keys1, keys2, expert_u, expert_v):
    b_, s_, d = h.shape
    t = b_ * s_
    hf = h.reshape(t, d)
    q = (hf @ w_query).reshape(t, PEER_HEADS, 2, PEER_HALF)
    s1 = jnp.einsum('thc,hnc->thn', q[:, :, 0], keys1)
    s2 = jnp.einsum('thc,hnc->thn', q[:, :, 1], keys2)
    v1, i1 = lax.top_k(s1, PEER_TOPK)
    v2, i2 = lax.top_k(s2, PEER_TOPK)
    cand_s = (v1[..., :, None] + v2[..., None, :]).reshape(t, PEER_HEADS, PEER_TOPK * PEER_TOPK)
    cand_i = (i1[..., :, None] * PEER_NKEYS + i2[..., None, :]).reshape(t, PEER_HEADS, PEER_TOPK * PEER_TOPK)
    top_s, top_pos = lax.top_k(cand_s, PEER_TOPK)
    idx = jnp.take_along_axis(cand_i, top_pos, axis=-1)
    gate = jax.nn.softmax(top_s.astype(jnp.float32), axis=-1).astype(h.dtype)
    nb = t // PEER_BLOCK

    def block(args):
        hb, ib, gb = args
        act = jax.nn.gelu(jnp.einsum('thkd,td->thk', expert_u[ib], hb), approximate=False)
        return jnp.einsum('thk,thkd->td', gb * act, expert_v[ib])

    out = lax.map(block, (hf.reshape(nb, PEER_BLOCK, d),
                          idx.reshape(nb, PEER_BLOCK, PEER_HEADS, PEER_TOPK),
                          gate.reshape(nb, PEER_BLOCK, PEER_HEADS, PEER_TOPK)))
    return out.reshape(b_, s_, d)

def second_inputs(seed: int = 0) -> dict:
    key = jax.random.key(seed)
    ks = jax.random.split(key, 18)
    f32 = jnp.float32
    nrm = lambda k, shape, scale: jax.random.normal(k, shape, f32) * scale
    gain = lambda k, shape: 1.0 + 0.02 * jax.random.normal(k, shape, f32)
    return {
        "x": jax.random.normal(ks[0], (BATCH, SEQ, D_MODEL), f32),
        "norm_mix_g": gain(ks[1], (DEPTH, D_MODEL)),
        "w_in": nrm(ks[2], (DEPTH, D_MODEL, IN_COLS), D_MODEL ** -0.5),
        "hg_lb_logits": nrm(ks[3], (DEPTH + 1, HG_WIDTH), 0.1),
        "hg_out_norm_g": gain(ks[4], (DEPTH, HG_WIDTH)),
        "conv_w": nrm(ks[5], (DEPTH, CONV_K, CONV_WIDTH), CONV_K ** -0.5),
        "w_branch_hg": nrm(ks[6], (DEPTH, HG_WIDTH, D_MODEL), HG_WIDTH ** -0.5),
        "w_branch_conv": nrm(ks[7], (DEPTH, CONV_WIDTH, D_MODEL), CONV_WIDTH ** -0.5),
        "w_out": nrm(ks[8], (DEPTH, D_MODEL, D_MODEL), D_MODEL ** -0.5),
        "norm_ffn_g": gain(ks[9], (DEPTH, D_MODEL)),
        "peer_w_query": nrm(ks[10], (DEPTH, D_MODEL, PEER_HEADS * PEER_QDIM), D_MODEL ** -0.5),
        "peer_keys1": nrm(ks[11], (DEPTH, PEER_HEADS, PEER_NKEYS, PEER_HALF), PEER_HALF ** -0.5),
        "peer_keys2": nrm(ks[12], (DEPTH, PEER_HEADS, PEER_NKEYS, PEER_HALF), PEER_HALF ** -0.5),
        "peer_u": nrm(ks[13], (DEPTH, PEER_N, D_MODEL), D_MODEL ** -0.5),
        "peer_v": nrm(ks[14], (DEPTH, PEER_N, D_MODEL), PEER_HEADS ** -0.5),
        "norm_final_g": gain(ks[15], (D_MODEL,)),
    }

def second_block(x, norm_mix_g, w_in, hg_lb_logits, hg_out_norm_g, conv_w, w_branch_hg,
              w_branch_conv, w_out, norm_ffn_g, peer_w_query, peer_keys1, peer_keys2,
              peer_u, peer_v, norm_final_g):
    b_, s_, _ = x.shape
    lb_all = jnp.cumsum(jax.nn.softmax(hg_lb_logits.astype(jnp.float32), axis=0), axis=0)
    split_at = list(np.cumsum(IN_SPLITS)[:-1])
    for l in range(DEPTH):
        h = rmsnorm_2(x, norm_mix_g[l])
        proj = h @ w_in[l]
        hq, hf, hi, hg, cb, cc, ch, gates = jnp.split(proj, split_at, axis=-1)

        lb = lb_all[l]
        q = jax.nn.silu(hq.astype(jnp.float32)) * (HG_DK ** -0.5)
        sig = jax.nn.sigmoid(hf.astype(jnp.float32))
        forget = lb + (1.0 - lb) * sig
        k = 1.0 - forget
        log_f = jnp.log(forget)
        rs = lambda t: t.reshape(b_, s_, HG_HEADS, -1)
        o = hgrn2_chunkwise(rs(q), rs(k), rs(log_f), rs(hi))
        o = o * lax.rsqrt(jnp.mean(o * o, axis=-1, keepdims=True) + EPS)
        o = o * hg_out_norm_g[l].astype(jnp.float32).reshape(HG_HEADS, HG_DV)
        y_a = (o.reshape(b_, s_, HG_WIDTH) * jax.nn.silu(hg.astype(jnp.float32))).astype(x.dtype)

        y_b = cb * causal_depthwise_conv(cc * ch, conv_w[l])

        g_a, g_b = jnp.split(jax.nn.sigmoid(gates), 2, axis=-1)
        merged = g_a * (y_a @ w_branch_hg[l]) + g_b * (y_b @ w_branch_conv[l])
        x = x + merged @ w_out[l]

        x = x + peer_ffn(rmsnorm_2(x, norm_ffn_g[l]), peer_w_query[l], peer_keys1[l],
                         peer_keys2[l], peer_u[l], peer_v[l])
    return rmsnorm_2(x, norm_final_g)


def setup_inputs(seed=0):
    out = dict(first_inputs(seed))
    for name, value in second_inputs(seed + 1).items():
        if name != "x":
            out[name + "_2"] = value
    return out


def reference(
    x, meta_tokens, mix_norm, w_in, gla_w_a2, gla_b_a, gla_out_norm, mla_q_norm, mla_w_qb,
    mla_kv_norm, mla_w_kvb, w_out, ffn_norm, router_group_w, router_group_b, router_expert_w,
    router_expert_b, expert_w_gate, expert_w_up, expert_w_down, final_norm, norm_mix_g_2,
    w_in_2, hg_lb_logits_2, hg_out_norm_g_2, conv_w_2, w_branch_hg_2, w_branch_conv_2, w_out_2,
    norm_ffn_g_2, peer_w_query_2, peer_keys1_2, peer_keys2_2, peer_u_2, peer_v_2,
    norm_final_g_2,
):
    x = first_block(
        x, meta_tokens, mix_norm, w_in, gla_w_a2, gla_b_a, gla_out_norm, mla_q_norm, mla_w_qb,
        mla_kv_norm, mla_w_kvb, w_out, ffn_norm, router_group_w, router_group_b,
        router_expert_w, router_expert_b, expert_w_gate, expert_w_up, expert_w_down, final_norm,
    )
    return second_block(
        x, norm_mix_g_2, w_in_2, hg_lb_logits_2, hg_out_norm_g_2, conv_w_2, w_branch_hg_2,
        w_branch_conv_2, w_out_2, norm_ffn_g_2, peer_w_query_2, peer_keys1_2, peer_keys2_2,
        peer_u_2, peer_v_2, norm_final_g_2,
    )


_drawn_inputs = setup_inputs


def setup_inputs(seed=0):
    import zlib

    import numpy as np

    out = dict(_drawn_inputs(seed))
    spreads = {}
    factors = {'mla_q_norm': 4.65,
     'mla_kv_norm': 3.791,
     'router_group_b': 11.61,
     'router_expert_b': 12.656,
     'hg_lb_logits_2': 4.142,
     'hg_out_norm_g_2': 12.171,
     'norm_final_g_2': 23.859,
     'gla_b_a': 3.236,
     'gla_out_norm': 6.238,
     'ffn_norm': 3.574,
     'norm_ffn_g_2': 10.805}
    for name, (base, spread) in spreads.items():
        noise = np.random.default_rng([zlib.crc32(name.encode()), seed]).standard_normal(out[name].shape)
        drawn = base * np.exp(spread * noise) if base else spread * noise
        out[name] = __import__('jax').numpy.asarray(drawn.astype(out[name].dtype))
    for name, factor in factors.items():
        out[name] = (out[name] * factor).astype(out[name].dtype)
    return out
```

```python
from contextlib import ExitStack

import numpy as np

import concourse.bass as bass
from concourse import mybir

F32 = mybir.dt.float32
U32 = mybir.dt.uint32
I32 = mybir.dt.int32
ACT = mybir.ActivationFunctionType
ALU = mybir.AluOpType
AX = mybir.AxisListType

P = 128
D = 1024
KD = D // P
SEQ = 512
META = 16
L = META + SEQ
NT = SEQ // P
EPS = 1e-6
CHUNK = 64
MAIN = slice(META, L)
PIECES = (slice(0, META), MAIN)
GLA_H, GLA_DK, GLA_DV, GLA_TAU, GATE_RANK = 4, 64, 128, 16.0, 16
MLA_H, NOPE, ROPE, MLA_V = 4, 128, 64, 128
N_GROUPS, PER_GROUP, D_EXPERT = 8, 8, 512
N_EXPERTS = N_GROUPS * PER_GROUP
KE = D_EXPERT // P
SLOTS = 64
SPILL = (2 * SEQ - 1) // SLOTS
MOE_BLOCKS = N_EXPERTS + SPILL + 1
HG_H, HG_D = 8, 64
HG_W = HG_H * HG_D
KH = HG_W // P
PEER_H, NKEYS, TOPK = 8, 128, 16
GROUP = 8
N_PASS = NKEYS // GROUP
LEVELS = (32, 16, 8, 4, 2, 1)

VEC = {}


def _vec(names):
    at = 0
    for name, width in names:
        VEC[name] = slice(at, at + width)
        at += width
    return at


VEC_W = _vec([("mix", KD), ("ffn", KD), ("final", KD), ("mix2", KD), ("ffn2", KD), ("final2", KD),
              ("qn", 2), ("kvn", 1), ("gla_out", GLA_H), ("b_a", 2), ("hg_out", KH),
              ("lb0", KH), ("lb1", KH), ("conv", 3 * KH)])


class Chain:

    def __init__(self, engine, sem):
        self.engine, self.sem, self.n = engine, sem, 0

    def __call__(self, instruction):
        self.n += 1
        instruction.then_inc(self.sem, 1)
        self.engine.wait_ge(self.sem, self.n)


class Core:

    def __init__(self, nc, stack):
        self.nc, self.stack = nc, stack
        self.psum = stack.enter_context(nc.psum_tensor("psum", [P, 8, 512], F32))
        self.sems = []

    def sem(self, name):
        self.sems.append(self.nc.alloc_semaphore(name=name))
        return self.sems[-1]

    def recycle(self):
        self.nc.clear_and_free_semaphores(self.sems)
        self.sems = []
        self.nc.all_engine_barrier()

    def sb(self, name, shape, dt=F32):
        return self.stack.enter_context(self.nc.sbuf_tensor("sb_" + name, shape, dt))

    def stage(self, name):
        return Stage(self, name)


class Stage:

    def __init__(self, core, name):
        self.core, self.name = core, name

    def __enter__(self):
        self.stack = ExitStack()
        return self

    def __exit__(self, *a):
        return self.stack.__exit__(*a)

    def sb(self, name, shape, dt=F32):
        return self.stack.enter_context(self.core.nc.sbuf_tensor(f"{self.name}_{name}", shape, dt))

    def sem(self, name):
        return self.core.sem(f"{self.name}_{name}")


def norm(core, name, src, dst, gain, dim, pieces=(slice(0, SEQ),)):
    nc, ps = core.nc, core.psum
    nk = src.shape[1]
    width = src.shape[2]
    with core.stage(name) as st:
        sq = st.sb("sq", [P, nk, width])
        mean = st.sb("mean", [P, width])
        inv = st.sb("inv", [P, width])
        rs = st.sb("rs", [P, width])
        sq_ready, ss_ready = st.sem("sq"), st.sem("ss")
        inv_ready, rs_ready, own = st.sem("inv"), st.sem("rs"), st.sem("own")
        with nc.Block() as block:
            @block.scalar
            def _(act):
                for k in range(nk):
                    act.activation(sq[:, k], src[:, k], ACT.Square).then_inc(sq_ready, 1)
                act.wait_ge(inv_ready, 1)
                act.activation(rs[:], inv[:], ACT.Sqrt).then_inc(rs_ready, 1)

            @block.tensor
            def _(pe):
                for k in range(nk):
                    pe.wait_ge(sq_ready, k + 1)
                    for b, c in enumerate(pieces):
                        last = nc.tensor.matmul(ps[:, b, 0:c.stop - c.start], core.ones[:], sq[:, k, c],
                                                start=k == 0, stop=k == nk - 1)
                last.then_inc(ss_ready, 1)

            @block.vector
            def _(dve):
                step = Chain(dve, own)
                dve.wait_ge(ss_ready, 1)
                for b, c in enumerate(pieces):
                    step(dve.tensor_scalar(mean[:, c], ps[:, b, 0:c.stop - c.start], 1.0 / dim, EPS,
                                           ALU.mult, ALU.add))
                dve.reciprocal(inv[:], mean[:]).then_inc(inv_ready, 1)
                dve.wait_ge(rs_ready, 1)
                for k in range(nk):
                    dve.scalar_tensor_tensor(out=dst[:, k], in0=src[:, k], scalar=gain[:, k:k + 1],
                                             in1=rs[:], op0=ALU.mult, op1=ALU.mult)


def project(core, name, w, rhs, n_tiles, pieces, finish, on_vector=False):
    nc, ps = core.nc, core.psum
    nk = rhs.shape[1]
    U = 4
    turns = n_tiles // U
    assert n_tiles % U == 0
    with core.stage(name) as st:
        wb = st.sb("w", [P, U, nk, P])
        w_ready = [st.sem(f"w{u}") for u in range(U)]
        summed = [st.sem(f"sum{u}") for u in range(U)]
        out_free = [st.sem(f"free{u}") for u in range(U)]
        with nc.Block() as block:
            @block.sync
            def _(sp):
                with sp.Fori(0, turns) as t:
                    for u in range(U):
                        sp.wait_ge(summed[u], t)
                        sp.dma_start(wb[:, u], w[t * U + u]).then_inc(w_ready[u], 16)

            @block.tensor
            def _(pe):
                with pe.Fori(0, turns) as t:
                    for u in range(U):
                        pe.wait_ge(w_ready[u], 16 * t + 16)
                        pe.wait_ge(out_free[u], t)
                        for b, c in enumerate(pieces):
                            for k in range(nk):
                                last = nc.tensor.matmul(ps[:, u + 4 * b, 0:c.stop - c.start], wb[:, u, k],
                                                        rhs[:, k, c], start=k == 0, stop=k == nk - 1)
                        last.then_inc(summed[u], 1)

            def empty(engine):
                with engine.Fori(0, turns) as t:
                    for u in range(U):
                        engine.wait_ge(summed[u], t + 1)
                        for b, c in enumerate(pieces):
                            last = finish(engine, t * U + u, ps[:, u + 4 * b, 0:c.stop - c.start], c)
                        last.then_inc(out_free[u], 1)

            if on_vector:
                @block.vector
                def _(dve):
                    empty(dve)
            else:
                @block.scalar
                def _(act):
                    empty(act)


def setup(core, A):
    nc = core.nc
    core.h = core.sb("h", [P, KD, L])
    core.ones = core.sb("ones", [P, P])
    core.ident = core.sb("ident", [P, P])
    core.vec = core.sb("vec", [P, VEC_W])
    loaded = core.sem("setup_loaded")
    with nc.Block() as block:
        @block.sync
        def _(sp):
            sp.dma_start(core.h[:], A["xT"]).then_inc(loaded, 16)
            sp.dma_start(core.vec[:], A["vectors"]).then_inc(loaded, 16)
            sp.dma_start(core.ident[:], A["ident"]).then_inc(loaded, 16)
            sp.wait_ge(loaded, 48)

        @block.gpsimd
        def _(pool):
            pool.memset(core.ones[:], 1.0)


def by_token(core, name, w, xn, out, tiles, extra=None):
    nc, ps = core.nc, core.psum
    nk, width = w.shape[1], w.shape[2]
    with core.stage(name) as st:
        wb = st.sb("w", [P, nk, width])
        w_ready, summed, copied = st.sem("w"), st.sem("sum"), st.sem("copied")
        if extra:
            xw = st.sb("xw", [P, nk, extra[0].shape[2]])
            m = extra[0].shape[2]
        with nc.Block() as block:
            @block.sync
            def _(sp):
                sp.dma_start(wb[:], w).then_inc(w_ready, 16)
                if extra:
                    sp.dma_start(xw[:], extra[0]).then_inc(w_ready, 16)

            @block.tensor
            def _(pe):
                pe.wait_ge(w_ready, 32 if extra else 16)
                for i, c0, n in tiles:
                    for k in range(nk):
                        last = nc.tensor.matmul(ps[0:n, i, 0:width], xn[:, k, c0:c0 + n], wb[:, k],
                                                start=k == 0, stop=k == nk - 1)
                    last.then_inc(summed, 1)
                if extra:
                    for b, c in enumerate(extra[2]):
                        for k in range(nk):
                            last = nc.tensor.matmul(ps[0:m, 6 + b, 0:c.stop - c.start], xw[:, k], xn[:, k, c],
                                                    start=k == 0, stop=k == nk - 1)
                    last.then_inc(summed, 1)

            @block.scalar
            def _(act):
                for j, (i, c0, n) in enumerate(tiles):
                    act.wait_ge(summed, j + 1)
                    act.activation(out[0:n, i], ps[0:n, i, 0:width], ACT.Copy)
                if extra:
                    act.wait_ge(summed, len(tiles) + 1)
                    for b, c in enumerate(extra[2]):
                        act.activation(extra[1][:, c], ps[0:m, 6 + b, 0:c.stop - c.start], ACT.Copy)


def gla(core, A, zT, v, a_low, y):
    nc, ps, vec, ident = core.nc, core.psum, core.vec, core.ident
    PAIRS, NC = 2, SEQ // CHUNK
    with core.stage("gla") as st:
        wa2 = st.sb("wa2", [GATE_RANK, 2 * P])
        reset = st.sb("reset", [P, L])
        mask = st.sb("mask", [P, P])
        t1, t2, ls, b = (st.sb(n, [P, PAIRS, L]) for n in ("t1", "t2", "ls", "b"))
        eb, enb, ed = (st.sb(n, [P, PAIRS, L]) for n in ("eb", "enb", "ed"))
        qe, ke, kd = (st.sb(n, [P, PAIRS, L]) for n in ("qe", "ke", "kd"))
        kdt = st.sb("kdt", [P, NT + 1, PAIRS * P])
        att = st.sb("att", [P, NT, GLA_H, P])
        state = st.sb("state", [P, PAIRS, NC, 2 * GLA_DV])
        loaded, gate_ps, lsig, decay = st.sem("loaded"), st.sem("gate"), st.sem("lsig"), st.sem("decay")
        acts, dves, logit_ready = st.sem("acts"), st.sem("dves"), st.sem("logit")
        b_ready, e_ready, k_ready = st.sem("b"), st.sem("e"), st.sem("k")
        kt_ps, kt_ready, u_ps, state_ready = st.sem("ktps"), st.sem("kt"), st.sem("u"), st.sem("state")
        s_ps, s_ready, o_ps = st.sem("sps"), st.sem("s"), st.sem("o")
        sq_ready, ss_ps, rs_ready, inv_ready, silu_ready = (
            st.sem(n) for n in ("sq", "ss", "rs", "inv", "silu"))

        def update_at(j):
            n = j if j < 2 else (j + 1) // 2 if j % 2 else 5 + j // 2
            return ps[:, n // 2, (n % 2) * 256:(n % 2) * 256 + 256]

        with nc.Block() as block:
            @block.sync
            def _(sp):
                sp.dma_start(wa2[:], A["w_a2"]).then_inc(loaded, 16)
                sp.dma_start(reset[:], A["reset"]).then_inc(loaded, 16)
                sp.dma_start(mask[:], A["chunk_causal"]).then_inc(loaded, 16)

            @block.tensor
            def _(pe):
                pe.wait_ge(loaded, 48)
                for p in range(PAIRS):
                    for j, c in enumerate(PIECES):
                        last = nc.tensor.matmul(ps[:, 2 * p + j, 0:c.stop - c.start], wa2[:, p * P:(p + 1) * P],
                                                a_low[:, c], start=True, stop=True)
                last.then_inc(gate_ps, 1)
                pe.wait_ge(k_ready, 1)
                for i in range(NT + 1):
                    n, c0 = (P, META + P * i) if i < NT else (META, 0)
                    for p in range(PAIRS):
                        last = nc.tensor.transpose(ps[0:n, 4 + i // 2, (i % 2) * 256 + p * P:(i % 2) * 256 + (p + 1) * P],
                                                   kd[:, p, c0:c0 + n], ident[:])
                last.then_inc(kt_ps, 1)
                pe.wait_ge(kt_ready, 1)
                for p in range(PAIRS):
                    if p:
                        pe.wait_ge(state_ready, p)
                    for j in range(NC):
                        if j == 0:
                            rows, tile = slice(0, META), NT
                        else:
                            rows, tile = slice(CHUNK * ((j - 1) % 2), CHUNK * ((j - 1) % 2) + CHUNK), (j - 1) // 2
                        last = nc.tensor.matmul(update_at(j), kdt[rows, tile, p * P:(p + 1) * P],
                                                v[rows, tile, p * 256:(p + 1) * 256], start=True, stop=True)
                    last.then_inc(u_ps, 1)
                pe.wait_ge(state_ready, PAIRS)
                for i in range(NT):
                    if i >= 2:
                        pe.wait_ge(s_ready, 2 * (i - 1))
                    c = slice(META + P * i, META + P * (i + 1))
                    for h in range(GLA_H):
                        r = slice(64 * (h % 2), 64 * (h % 2) + 64)
                        last = nc.tensor.matmul(ps[:, 4 + 2 * (i % 2) + h % 2, (h // 2) * P:(h // 2 + 1) * P], ke[r, h // 2, c],
                                                qe[r, h // 2, c], start=True, stop=True)
                    last.then_inc(s_ps, 1)
                pe.wait_ge(s_ready, 2 * NT)
                for h in range(GLA_H):
                    r = slice(64 * (h % 2), 64 * (h % 2) + 64)
                    for i in range(NT):
                        nc.tensor.matmul(ps[:, h, i * P:(i + 1) * P], v[:, i, h * P:(h + 1) * P],
                                         att[:, i, h], start=True, stop=False)
                        for j in (2 * i, 2 * i + 1):
                            last = nc.tensor.matmul(ps[:, h, j * CHUNK:(j + 1) * CHUNK],
                                                    state[r, h // 2, j, (h % 2) * P:(h % 2) * P + P],
                                                    qe[r, h // 2, META + j * CHUNK:META + (j + 1) * CHUNK],
                                                    start=False, stop=j == 2 * i + 1)
                    last.then_inc(o_ps, 1)
                for h in range(GLA_H):
                    pe.wait_ge(sq_ready, h + 1)
                    nc.tensor.matmul(ps[:, 4 + h], core.ones[:], t1[:, h // 2, 0:SEQ] if h % 2 == 0 else t2[:, h // 2, 0:SEQ],
                                     start=True, stop=True).then_inc(ss_ps, 1)

            @block.scalar
            def _(act):
                step = Chain(act, acts)
                act.wait_ge(logit_ready, 2 * PAIRS)
                step(act.activation(t1[:], kd[:], ACT.Abs))
                step(act.activation(t2[:], t1[:], ACT.Exp, scale=-1.0))
                act.activation(ls[:], t2[:], ACT.Ln, bias=1.0).then_inc(lsig, 1)
                act.wait_ge(b_ready, 1)
                act.activation(eb[:], b[:], ACT.Exp, scale=1.0 / GLA_TAU)
                act.activation(enb[:], b[:], ACT.Exp, scale=-1.0 / GLA_TAU)
                act.activation(ed[:], t1[:], ACT.Exp, scale=1.0 / GLA_TAU).then_inc(e_ready, 1)
                act.activation(zT[:, 4:8], zT[:, 4:8], ACT.Silu).then_inc(silu_ready, 1)
                act.wait_ge(k_ready, 1)
                for h in range(GLA_H):
                    act.wait_ge(o_ps, h + 1)
                    act.activation(t1[:, h // 2, 0:SEQ] if h % 2 == 0 else t2[:, h // 2, 0:SEQ],
                                   ps[:, h], ACT.Square).then_inc(sq_ready, 1)
                for h in range(GLA_H):
                    act.wait_ge(inv_ready, h + 1)
                    act.activation(enb[:, h // 2, 0:SEQ] if h % 2 == 0 else eb[:, h // 2, 0:SEQ],
                                   ed[:, h // 2, 0:SEQ] if h % 2 == 0 else kd[:, h // 2, 0:SEQ],
                                   ACT.Sqrt).then_inc(rs_ready, 1)

            @block.vector
            def _(dve):
                step = Chain(dve, dves)
                dve.wait_ge(gate_ps, 1)
                for p in range(PAIRS):
                    for j, c in enumerate(PIECES):
                        dve.tensor_scalar(kd[:, p, c], ps[:, 2 * p + j, 0:c.stop - c.start],
                                          vec[:, VEC["b_a"]][:, p:p + 1], None, ALU.add).then_inc(logit_ready, 1)
                dve.wait_ge(logit_ready, 2 * PAIRS)
                step(dve.tensor_scalar(qe[:], kd[:], 0.0, None, ALU.min))
                dve.wait_ge(lsig, 1)
                step(dve.tensor_tensor(ke[:], qe[:], ls[:], ALU.subtract))
                for p in range(PAIRS):
                    step(dve.tensor_tensor_scan(b[:, p], reset[:], ke[:, p], 0.0, ALU.mult, ALU.add))
                step(dve.tensor_tensor(t1[:, :, 0:META],
                                       b[:, :, META - 1:META].to_broadcast([P, PAIRS, META]),
                                       b[:, :, 0:META], ALU.subtract))
                for p in range(PAIRS):
                    bm = b[:, p, MAIN].rearrange("p (n c) -> p n c", c=CHUNK)
                    step(dve.tensor_tensor(t1[:, p, MAIN].rearrange("p (n c) -> p n c", c=CHUNK),
                                           bm[:, :, CHUNK - 1:CHUNK].to_broadcast([P, NC, CHUNK]),
                                           bm, ALU.subtract))
                dve.sem_inc(b_ready, 1)
                dve.wait_ge(e_ready, 1)
                dve.scalar_tensor_tensor(out=qe[:], in0=zT[:, 0:2], scalar=float(GLA_DK) ** -0.5, in1=eb[:],
                                         op0=ALU.mult, op1=ALU.mult)
                dve.tensor_tensor(ke[:], zT[:, 2:4], enb[:], ALU.mult)
                step(dve.tensor_tensor(kd[:], zT[:, 2:4], ed[:], ALU.mult))
                dve.sem_inc(k_ready, 1)
                dve.wait_ge(kt_ps, 1)
                for i in range(NT + 1):
                    n = P if i < NT else META
                    step(dve.tensor_copy(kdt[0:n, i], ps[0:n, 4 + i // 2, (i % 2) * 256:(i % 2) * 256 + 256]))
                dve.sem_inc(kt_ready, 1)
                for p in range(PAIRS):
                    dve.wait_ge(u_ps, p + 1)
                    step(dve.tensor_copy(state[:, p, 0], update_at(0)))
                    for j in range(1, NC):
                        end = META + j * CHUNK - 1
                        step(dve.scalar_tensor_tensor(out=state[:, p, j], in0=state[:, p, j - 1],
                                                      scalar=eb[:, p, end:end + 1],
                                                      in1=update_at(j),
                                                      op0=ALU.mult, op1=ALU.add))
                    dve.sem_inc(state_ready, 1)
                for i in range(NT):
                    dve.wait_ge(s_ps, i + 1)
                    for half in range(2):
                        dve.tensor_tensor(att[:, i, half::2],
                                          ps[:, 4 + 2 * (i % 2) + half, 0:2 * P].rearrange("p (h c) -> p h c", c=P),
                                          mask[:].unsqueeze(1).to_broadcast([P, 2, P]), ALU.mult).then_inc(s_ready, 1)
                for h in range(GLA_H):
                    mean = (b if h % 2 == 0 else ls)[:, h // 2, 0:SEQ]
                    dve.wait_ge(ss_ps, h + 1)
                    step(dve.tensor_scalar(mean, ps[:, 4 + h], 1.0 / GLA_DV, EPS, ALU.mult, ALU.add))
                    dve.reciprocal(ed[:, h // 2, 0:SEQ] if h % 2 == 0 else kd[:, h // 2, 0:SEQ],
                                   mean).then_inc(inv_ready, 1)
                dve.wait_ge(silu_ready, 1)
                for h in range(GLA_H):
                    rs = enb[:, h // 2, 0:SEQ] if h % 2 == 0 else eb[:, h // 2, 0:SEQ]
                    dve.wait_ge(rs_ready, h + 1)
                    step(dve.scalar_tensor_tensor(out=y[:, h], in0=ps[:, h], scalar=vec[:, VEC["gla_out"]][:, h:h + 1],
                                                  in1=rs, op0=ALU.mult, op1=ALU.mult))
                    step(dve.tensor_tensor(y[:, h], y[:, h], zT[:, 4 + h, MAIN], ALU.mult))


def mla(core, A, zT, y):
    nc, ps, vec, ident = core.nc, core.psum, core.vec, core.ident
    SCALE = float(NOPE + ROPE) ** -0.5
    with core.stage("mla") as st:
        qn, kvn = st.sb("qn", [P, 2, SEQ]), st.sb("kvn", [P, 1, L])
        norm(core, "mla_nq", zT[:, 8:10, MAIN], qn, vec[:, VEC["qn"]], 2 * P)
        norm(core, "mla_nkv", zT[:, 10:11], kvn, vec[:, VEC["kvn"]], P, PIECES)
        wq = st.sb("wq", [P, 2, 6, P])
        wkv = st.sb("wkv", [P, 2, 4 * P])
        cs, sn, rot = st.sb("cos", [P, L]), st.sb("sin", [P, L]), st.sb("rot", [P, P])
        q = st.sb("q", [P, 6, SEQ])
        kn = st.sb("kn", [P, MLA_H, L])
        kr = st.sb("kr", [P, L])
        v = st.sb("v", [P, NT + 1, 4 * P])
        rt = st.sb("rt", [P, 3, L])
        loaded, q_ps, q_out, k_ps, k_out, v_ps, v_out = (st.sem(n) for n in ("ld", "qp", "qo", "kp", "ko", "vp", "vo"))
        r_ps, dves = st.sem("rp"), st.sem("dv")
        with nc.Block() as block:
            @block.sync
            def _(sp):
                for dst, src in ((wq, "w_qb"), (wkv, "w_kvb"), (cs, "rope_cos"), (sn, "rope_sin"), (rot, "rope_rot")):
                    sp.dma_start(dst[:], A[src]).then_inc(loaded, 16)

            @block.tensor
            def _(pe):
                pe.wait_ge(loaded, 80)
                for m in range(6):
                    if m >= 2:
                        pe.wait_ge(q_out, m - 1)
                    for k in range(2):
                        last = nc.tensor.matmul(ps[:, m % 2], wq[:, k, m], qn[:, k], start=k == 0, stop=k == 1)
                    last.then_inc(q_ps, 1)
                for h in range(MLA_H):
                    if h >= 1:
                        pe.wait_ge(k_out, h)
                    for j, c in enumerate(PIECES):
                        last = nc.tensor.matmul(ps[:, 2 + j, 0:c.stop - c.start], wkv[:, 0, h * P:(h + 1) * P],
                                                kvn[:, 0, c], start=True, stop=True)
                    last.then_inc(k_ps, 1)
                for i in range(NT + 1):
                    if i >= 2:
                        pe.wait_ge(v_out, i - 1)
                    n, c0 = (P, META + P * i) if i < NT else (META, 0)
                    nc.tensor.matmul(ps[0:n, 4 + i % 2], kvn[:, 0, c0:c0 + n], wkv[:, 1], start=True,
                                     stop=True).then_inc(v_ps, 1)
                pe.wait_ge(q_out, 6)
                pe.wait_ge(v_out, NT + 1)
                for m in range(2):
                    nc.tensor.matmul(ps[:, 4 + m], rot[:], q[:, 4 + m], start=True, stop=True)
                for j, c in enumerate(PIECES):
                    last = nc.tensor.matmul(ps[:, 6 + j, 0:c.stop - c.start], rot[:], zT[:, 11, c], start=True, stop=True)
                last.then_inc(r_ps, 1)

            @block.scalar
            def _(act):
                for m in range(6):
                    act.wait_ge(q_ps, m + 1)
                    act.activation(q[:, m], ps[:, m % 2], ACT.Copy).then_inc(q_out, 1)
                for i in range(NT + 1):
                    n = P if i < NT else META
                    act.wait_ge(v_ps, i + 1)
                    act.activation(v[0:n, i], ps[0:n, 4 + i % 2], ACT.Copy).then_inc(v_out, 1)

            @block.vector
            def _(dve):
                for h in range(MLA_H):
                    dve.wait_ge(k_ps, h + 1)
                    dve.tensor_copy(kn[:, h, 0:META], ps[:, 2, 0:META])
                    dve.tensor_copy(kn[:, h, MAIN], ps[:, 3]).then_inc(k_out, 1)
                step = Chain(dve, dves)
                dve.wait_ge(loaded, 80)
                dve.wait_ge(r_ps, 1)
                for m in range(2):
                    step(dve.tensor_tensor(rt[:, m, 0:SEQ], ps[:, 4 + m], sn[:, MAIN], ALU.mult))
                    step(dve.tensor_tensor(q[:, 4 + m], q[:, 4 + m], cs[:, MAIN], ALU.mult))
                    step(dve.tensor_tensor(q[:, 4 + m], q[:, 4 + m], rt[:, m, 0:SEQ], ALU.add))
                for j, c in enumerate(PIECES):
                    step(dve.tensor_tensor(rt[:, 2, c], ps[:, 6 + j, 0:c.stop - c.start], sn[:, c], ALU.mult))
                step(dve.tensor_tensor(kr[:], zT[:, 11], cs[:], ALU.mult))
                step(dve.tensor_tensor(kr[:], kr[:], rt[:, 2], ALU.add))

        prob = st.sb("prob", [P, 2, L])
        pT = st.sb("pT", [P, 2, NT + 1, P])
        stat = st.sb("stat", [P, 4, 16])
        s_ps, s_free, mx, ex, pn, t_ps, t_out, o_ps, o_out, dves2 = (
            st.sem(n) for n in ("s", "sf", "mx", "ex", "pn", "tp", "to", "op", "oo", "d2"))
        work = [(h, i) for h in range(MLA_H) for i in range(NT)]
        flat = ps[:].rearrange("p a b -> p (a b)")

        def scores_at(b):
            return 1024 * (b % 2) + 512 - META

        with nc.Block() as block:
            @block.tensor
            def _(pe):
                def scores(b):
                    h, i = work[b]
                    if b >= 2:
                        pe.wait_ge(ex, b - 1)
                    r = slice(64 * (h % 2), 64 * (h % 2) + 64)
                    qc = slice(P * i, P * (i + 1))
                    n = P * (i + 1)
                    base = scores_at(b)
                    for o, c in ((base, slice(0, META)), (base + META, slice(META, META + n))):
                        out = flat[:, o:o + c.stop - c.start]
                        nc.tensor.matmul(out, q[:, h, qc], kn[:, h, c], start=True, stop=False)
                        last = nc.tensor.matmul(out, q[r, 4 + h // 2, qc], kr[r, c], start=False, stop=True)
                    last.then_inc(s_ps, 1)

                scores(0)
                for b, (h, i) in enumerate(work):
                    if b + 1 < len(work):
                        scores(b + 1)
                    pe.wait_ge(pn, b + 1)
                    if b >= 1:
                        pe.wait_ge(t_out, b)
                    for j in range(i + 1):
                        nc.tensor.transpose(flat[:, 2048 + j * P:2048 + (j + 1) * P],
                                            prob[:, b % 2, META + j * P:META + (j + 1) * P], ident[:])
                    nc.tensor.transpose(flat[0:META, 2560:2560 + P], prob[:, b % 2, 0:META], ident[:]).then_inc(t_ps, 1)
                    pe.wait_ge(t_out, b + 1)
                    if b >= 2:
                        pe.wait_ge(o_out, b - 1)
                    out = ps[:, 6 + b % 2, 0:P]
                    nc.tensor.matmul(out, v[0:META, NT, h * P:(h + 1) * P], pT[0:META, b % 2, NT], start=True, stop=False)
                    for j in range(i + 1):
                        last = nc.tensor.matmul(out, v[:, j, h * P:(h + 1) * P], pT[:, b % 2, j],
                                                start=False, stop=j == i)
                    last.then_inc(o_ps, 1)

            @block.vector
            def _(dve):
                step = Chain(dve, dves2)
                for b, (h, i) in enumerate(work):
                    n = META + P * (i + 1)
                    base = scores_at(b)
                    dve.wait_ge(s_ps, b + 1)
                    step(dve.memset(flat[0:CHUNK, base + n - CHUNK:base + n], -3.0e38))
                    step(dve.tensor_reduce(stat[:, 0, b:b + 1], flat[:, base:base + n], AX.X, ALU.max))
                    dve.tensor_scalar(stat[:, 1, b:b + 1], stat[:, 0, b:b + 1], -SCALE, None, ALU.mult).then_inc(mx, 1)
                    dve.wait_ge(ex, b + 1)
                    step(dve.reciprocal(stat[:, 3, b:b + 1], stat[:, 2, b:b + 1]))
                    dve.tensor_scalar(prob[:, b % 2, 0:n], prob[:, b % 2, 0:n], stat[:, 3, b:b + 1], None,
                                      ALU.mult).then_inc(pn, 1)

            @block.scalar
            def _(act):
                def exponentials(b):
                    h, i = work[b]
                    n = META + P * (i + 1)
                    act.wait_ge(mx, b + 1)
                    if b >= 2:
                        act.wait_ge(t_ps, b - 1)
                    act.activation(prob[:, b % 2, 0:n], flat[:, scores_at(b):scores_at(b) + n], ACT.Exp,
                                   bias=stat[:, 1, b:b + 1], scale=SCALE,
                                   accum_out=stat[:, 2, b:b + 1]).then_inc(ex, 1)

                exponentials(0)
                for b, (h, i) in enumerate(work):
                    if b + 1 < len(work):
                        exponentials(b + 1)
                    act.wait_ge(t_ps, b + 1)
                    if b >= 2:
                        act.wait_ge(o_ps, b - 1)
                    act.activation(pT[:, b % 2, 0:i + 1],
                                   flat[:, 2048:2048 + P * (i + 1)].rearrange("p (j c) -> p j c", c=P), ACT.Copy)
                    act.activation(pT[0:META, b % 2, NT], flat[0:META, 2560:2560 + P], ACT.Copy).then_inc(t_out, 1)
                    act.wait_ge(o_ps, b + 1)
                    act.activation(y[:, 4 + h, i * P:(i + 1) * P], ps[:, 6 + b % 2, 0:P], ACT.Copy).then_inc(o_out, 1)


def first_mixer(core, A):
    with core.stage("mix1") as st:
        zT = st.sb("zT", [P, 12, L])
        v = st.sb("v", [P, NT + 1, 512])
        a_low = st.sb("a_low", [GATE_RANK, L])
        y = st.sb("y", [P, KD, SEQ])
        with core.stage("mix1n") as s2:
            xn = s2.sb("xn", [P, KD, L])
            norm(core, "n1", core.h, xn, core.vec[:, VEC["mix"]], D, PIECES)
            project(core, "in1", A["w_in"], xn, 12, PIECES,
                    lambda act, m, acc, c: act.activation(zT[:, m, c], acc, ACT.Copy))
            by_token(core, "in1v", A["w_v"], xn, v,
                     [(i, META + P * i, P) for i in range(NT)] + [(NT, 0, META)],
                     (A["w_alow"], a_low, PIECES))
        gla(core, A, zT, v, a_low, y)
        mla(core, A, zT, y)
        add_projection(core, "out1", A["w_out"], y)


def add_projection(core, name, w, y):
    project(core, name, w, y, KD, (slice(0, SEQ),),
            lambda dve, m, acc, c: dve.tensor_tensor(core.h[:, m, MAIN], core.h[:, m, MAIN], acc, ALU.add),
            on_vector=True)


def route(core, A, t, T_rows, slot_tok, slots_u, gates, block_tok, spill):
    nc, ps, ident = core.nc, core.psum, core.ident
    NB = MOE_BLOCKS
    NS = SPILL + 1
    NR = N_GROUPS + N_EXPERTS
    with core.stage("route") as st:
        wr, bias = st.sb("wr", [P, KD, NR]), st.sb("bias", [P, NR])
        tri, io, tok = st.sb("tri", [P, P]), st.sb("iota", [P, N_EXPERTS]), st.sb("tok", [P, NT], U32)
        zero = st.sb("zero", [P, NB * SLOTS // P], U32)
        rows = st.sb("rows", [P, NT, D])
        lg = st.sb("lg", [P, NT, NR])
        g8, gi = st.sb("g8", [P, NT, 8]), st.sb("gi", [P, NT, 8], U32)
        e8, ei = st.sb("e8", [P, NT, 8]), st.sb("ei", [P, NT, 8], U32)
        gd, gone = st.sb("gd", [P, NT, 8]), st.sb("gone", [P, NT, 8])
        gsum, gp = st.sb("gsum", [P, NT]), st.sb("gp", [P, NT])
        prod, el = st.sb("prod", [P, NT, PER_GROUP, N_GROUPS]), st.sb("el", [P, NT, PER_GROUP])
        gf, ef = st.sb("gf", [P, NT]), st.sb("ef", [P, NT, 2])
        ea, eo, er = st.sb("ea", [P, NT]), st.sb("eo", [P, NT]), st.sb("er", [P, NT])
        xf = st.sb("xf", [P, 2, NT])
        pick = st.sb("pick", [P, 2, NT, N_EXPERTS])
        both = st.sb("both", [P, NT, N_EXPERTS])
        cnt, nb, nbe, base = (st.sb(n, [P, N_EXPERTS]) for n in ("cnt", "nb", "nbe", "base"))
        rank, over = st.sb("rank", [P, NT, N_EXPERTS]), st.sb("over", [P, NT, N_EXPERTS])
        sl, slf = st.sb("sl", [P, 2, NT, N_EXPERTS]), st.sb("slf", [P, 2, NT])
        le, ex = st.sb("le", [P, NS, N_EXPERTS]), st.sb("ex", [P, NS + 1])
        loaded, log_ps, row_ps, row_free, row_out, saved = (st.sem(n) for n in ("ld", "lg", "rp", "rf", "ro", "sv"))
        own, a_in, a_out, pick_ready, rank_ps, slot_ready, zeroed = (
            st.sem(n) for n in ("own", "ai", "ao", "pk", "rk", "sr", "zd"))
        scattered = [st.sem(f"sc{n}") for n in range(2 * NT)]
        with nc.Block() as block:
            @block.sync
            def _(sp):
                for dst, src in ((wr, "w_router"), (bias, "b_router"), (tri, "before"), (io, "iota"), (tok, "tokens")):
                    sp.dma_start(dst[:], A[src]).then_inc(loaded, 16)
                sp.wait_ge(own, 1)
                sp.dma_start(slot_tok.rearrange("(p n) o -> p (n o)", p=P), zero[:]).then_inc(zeroed, 16)
                for i in range(NT):
                    sp.wait_ge(row_out, 2 * i + 2)
                sp.dma_start(T_rows.rearrange("(i p) d -> p i d", p=P), rows[:]).then_inc(saved, 16)
                sp.wait_ge(saved, 16)
                for n in range(2 * NT):
                    sp.wait_ge(scattered[n], 16)
                sp.dma_start(block_tok[:], slot_tok.rearrange("(b s) o -> s (b o)", s=SLOTS),
                             allow_slow_non_contiguous=True).then_inc(saved, 16)
                sp.wait_ge(saved, 32)

            @block.tensor
            def _(pe):
                pe.wait_ge(loaded, 80)
                for i in range(NT):
                    for k in range(KD):
                        last = nc.tensor.matmul(ps[:, 0, i * NR:(i + 1) * NR], t[:, k, i * P:(i + 1) * P], wr[:, k],
                                                start=k == 0, stop=k == KD - 1)
                last.then_inc(log_ps, 1)
                for i in range(NT):
                    if i >= 2:
                        pe.wait_ge(row_out, 2 * i - 2)
                    for k in range(KD):
                        last = nc.tensor.transpose(ps[:, 2 + 2 * (i % 2) + k // 4, (k % 4) * P:(k % 4 + 1) * P],
                                                   t[:, k, i * P:(i + 1) * P], ident[:])
                    last.then_inc(row_ps, 1)
                pe.wait_ge(pick_ready, 1)
                for i in range(NT):
                    for j in range(i + 1):
                        nc.tensor.matmul(ps[:, 1, i * N_EXPERTS:(i + 1) * N_EXPERTS], tri[:] if j == i else core.ones[:],
                                         both[:, j], start=j == 0, stop=j == i)
                for j in range(NT):
                    last = nc.tensor.matmul(ps[:, 1, NT * N_EXPERTS:(NT + 1) * N_EXPERTS], core.ones[:], both[:, j],
                                            start=j == 0, stop=j == NT - 1)
                last.then_inc(rank_ps, 1)

            @block.scalar
            def _(act):
                for i in range(NT):
                    act.wait_ge(row_ps, i + 1)
                    for b in range(2):
                        act.activation(rows[:, i, b * 512:(b + 1) * 512], ps[:, 2 + 2 * (i % 2) + b], ACT.Copy).then_inc(row_out, 1)
                act.wait_ge(a_in, 1)
                act.activation(gd[:], gone[:], ACT.Exp)
                act.activation(ea[:], er[:], ACT.Exp).then_inc(a_out, 1)

            @block.vector
            def _(dve):
                step = Chain(dve, own)
                step(dve.memset(zero[:], 0))
                dve.wait_ge(loaded, 80)
                dve.wait_ge(log_ps, 1)
                step(dve.tensor_tensor(lg[:], ps[:, 0, 0:NT * NR].rearrange("p (i n) -> p i n", n=NR),
                                       bias[:].unsqueeze(1).to_broadcast([P, NT, NR]), ALU.add))
                for i in range(NT):
                    step(dve.max(g8[:, i], lg[:, i, 0:8]))
                    step(dve.max_index(gi[:, i], g8[:, i], lg[:, i, 0:8]))
                step(dve.tensor_tensor(gone[:], lg[:, :, 0:8], g8[:, :, 0:1].to_broadcast([P, NT, 8]), ALU.subtract))
                step(dve.tensor_copy(gf[:], gi[:, :, 0]))
                for i in range(NT):
                    step(dve.tensor_scalar(over[:, i, 0:8], io[:, 0:8], gf[:, i:i + 1], None, ALU.is_equal))
                for i in range(NT):
                    step(dve.tensor_tensor(prod[:, i], lg[:, i, 8:].rearrange("p (g e) -> p e g", g=N_GROUPS),
                                           over[:, i, 0:8].unsqueeze(1).to_broadcast([P, PER_GROUP, N_GROUPS]), ALU.mult))
                step(dve.tensor_reduce(el[:], prod[:], AX.X, ALU.add))
                for i in range(NT):
                    step(dve.max(e8[:, i], el[:, i]))
                    step(dve.max_index(ei[:, i], e8[:, i], el[:, i]))
                step(dve.tensor_tensor(er[:], e8[:, :, 1], e8[:, :, 0], ALU.subtract))
                dve.sem_inc(a_in, 1)
                step(dve.tensor_copy(ef[:], ei[:, :, 0:2]))
                for j in range(2):
                    step(dve.scalar_tensor_tensor(out=xf[:, j], in0=gf[:], scalar=float(PER_GROUP), in1=ef[:, :, j],
                                                  op0=ALU.mult, op1=ALU.add))
                for j in range(2):
                    for i in range(NT):
                        step(dve.tensor_scalar(pick[:, j, i], io[:], xf[:, j, i:i + 1], None, ALU.is_equal))
                step(dve.tensor_tensor(both[:], pick[:, 0], pick[:, 1], ALU.add))
                dve.sem_inc(pick_ready, 1)
                dve.wait_ge(a_out, 1)
                step(dve.tensor_reduce(gsum[:], gd[:], AX.X, ALU.add))
                step(dve.reciprocal(gp[:], gsum[:]))
                step(dve.tensor_scalar(eo[:], ea[:], 1.0, None, ALU.add))
                step(dve.reciprocal(er[:], eo[:]))
                step(dve.tensor_tensor(gates[:, 0], gp[:], er[:], ALU.mult))
                step(dve.tensor_tensor(gates[:, 1], gates[:, 0], ea[:], ALU.mult))
                dve.wait_ge(rank_ps, 1)
                step(dve.tensor_copy(cnt[:], ps[:, 1, NT * N_EXPERTS:(NT + 1) * N_EXPERTS]))
                step(dve.tensor_scalar(nb[:], cnt[:], float(SLOTS), None, ALU.is_gt))
                for m in range(2, SEQ // SLOTS):
                    step(dve.scalar_tensor_tensor(out=nb[:], in0=cnt[:], scalar=float(m * SLOTS), in1=nb[:],
                                                  op0=ALU.is_gt, op1=ALU.add))
                step(dve.tensor_tensor_scan(nbe[:], core.ones[:, 0:N_EXPERTS], nb[:], 0.0, ALU.mult, ALU.add))
                step(dve.tensor_tensor(base[:], nbe[:], nb[:], ALU.subtract))
                step(dve.tensor_tensor(base[:], base[:], io[:], ALU.subtract))
                step(dve.tensor_scalar(base[:], base[:], float(SLOTS), float((N_EXPERTS - 1) * SLOTS), ALU.mult, ALU.add))
                step(dve.tensor_copy(rank[:], ps[:, 1, 0:NT * N_EXPERTS].rearrange("p (i e) -> p i e", e=N_EXPERTS)))
                step(dve.tensor_scalar(over[:], rank[:], float(SLOTS), None, ALU.is_ge))
                step(dve.tensor_tensor(over[:], over[:], base[:].unsqueeze(1).to_broadcast([P, NT, N_EXPERTS]), ALU.mult))
                step(dve.tensor_tensor(rank[:], rank[:], over[:], ALU.add))
                step(dve.tensor_scalar(cnt[:], io[:], float(SLOTS), None, ALU.mult))
                step(dve.tensor_tensor(rank[:], rank[:], cnt[:].unsqueeze(1).to_broadcast([P, NT, N_EXPERTS]), ALU.add))
                for j in range(2):
                    step(dve.tensor_tensor(sl[:, j], pick[:, j], rank[:], ALU.mult))
                step(dve.tensor_reduce(slf[:], sl[:], AX.X, ALU.add))
                step(dve.tensor_copy(slots_u[:], slf[:]))
                dve.sem_inc(slot_ready, 1)
                for b in range(NS):
                    step(dve.tensor_scalar(le[:, b], nbe[:], float(b), None, ALU.is_le))
                step(dve.tensor_reduce(ex[:, 0:NS], le[:], AX.X, ALU.add))
                step(dve.tensor_scalar(ex[:, 0:NS], ex[:, 0:NS], float(N_EXPERTS - 1), None, ALU.min))
                step(dve.tensor_copy(ex[:, NS:NS + 1], nbe[:, N_EXPERTS - 1:N_EXPERTS]))
                step(dve.tensor_copy(spill[:], ex[0:1, :]))

            @block.gpsimd
            def _(pool):
                pool.wait_ge(loaded, 80)
                pool.wait_ge(zeroed, 16)
                pool.wait_ge(slot_ready, 1)
                for j in range(2):
                    for i in range(NT):
                        pool.indirect_dma_start(
                            out=slot_tok, out_offset=bass.IndirectOffsetOnAxis(ap=slots_u[:, j, i:i + 1], axis=0),
                            in_=tok[:, i:i + 1], in_offset=None).then_inc(scattered[j * NT + i], 16)
                for n in range(2 * NT):
                    pool.wait_ge(scattered[n], 16)


def experts(core, A, T_rows, Y_rows, block_tok, spill):
    nc, ps, ident = core.nc, core.psum, core.ident
    H, F = 2, D_EXPERT
    w_gate, w_up, w_down = A["w_gate"], A["w_up"], A["w_down"]
    with core.stage("moe") as st:
        wg, wu = st.sb("wg", [P, H, KD, F]), st.sb("wu", [P, H, KD, F])
        wd = st.sb("wd", [P, H, KE, D])
        idx = [st.sb(f"idx{u}", [SLOTS, 1], U32) for u in range(H)]
        xg = st.sb("xg", [SLOTS, H, D])
        xT = st.sb("xT", [P, H, KD, SLOTS])
        sg, hd = st.sb("sg", [SLOTS, H, F]), st.sb("hd", [SLOTS, H, F])
        hT = st.sb("hT", [P, H, KE, SLOTS])
        yo = st.sb("yo", [SLOTS, H, D])
        cleared = st.sem("cleared")
        opened = st.sem("opened")
        gate_pool, gate_pe, gate_act_end = st.sem("gpool"), st.sem("gpe"), st.sem("gact")
        names = ("wgu", "wd", "idx", "xg", "xps", "xT", "gu", "sg", "hd", "hps", "hT", "dn", "yo", "ys")
        S = {n: [st.sem(f"{n}{u}") for u in range(H)] for n in names}

        zero = st.sb("zero", [SLOTS, D])

        def expert_weights(sp, e, u):
            sp.dma_start(wg[:, u], w_gate[e]).then_inc(S["wgu"][u], 16)
            sp.dma_start(wu[:, u], w_up[e]).then_inc(S["wgu"][u], 16)

        def down_weights(sp, e, u):
            sp.dma_start(wd[:, u], w_down[e]).then_inc(S["wd"][u], 16)

        def gather(pool, column, u, n):
            pool.wait_ge(S["xg"][u], 16 * n)
            pool.tensor_copy(idx[u][:], block_tok[:, column]).then_inc(S["idx"][u], 1)
            pool.wait_ge(S["idx"][u], n + 1)
            pool.wait_ge(S["xps"][u], n)
            pool.sem_inc(gate_pool, 1)
            pool.indirect_dma_start(out=xg[:, u], out_offset=None, in_=T_rows,
                                    in_offset=bass.IndirectOffsetOnAxis(ap=idx[u][:, 0:1], axis=0)
                                    ).then_inc(S["xg"][u], 16)

        def turn_tokens(pe, u, n, n_other):
            pe.wait_ge(S["xg"][u], 16 * n + 16)
            pe.wait_ge(S["xT"][1 - u], n_other)
            pe.sem_inc(gate_pe, 1)
            for k in range(KD):
                last = nc.tensor.transpose(ps[:, 0, k * SLOTS:(k + 1) * SLOTS], xg[:, u, k::KD],
                                           ident[0:SLOTS, 0:SLOTS])
            last.then_inc(S["xps"][u], 1)

        def gate_up(pe, u, n):
            pe.wait_ge(S["wgu"][u], 32 * n + 32)
            pe.wait_ge(S["xT"][u], n + 1)
            pe.wait_ge(S["hd"][u], n)
            for w, bank in ((wg, 2 + u), (wu, 4 + u)):
                for k in range(KD):
                    last = nc.tensor.matmul(ps[0:SLOTS, bank], xT[:, u, k], w[:, u, k], start=k == 0, stop=k == KD - 1)
            last.then_inc(S["gu"][u], 1)

        def turn_hidden(pe, u, n, n_other):
            pe.wait_ge(S["hd"][u], n + 1)
            pe.wait_ge(S["hT"][1 - u], n_other)
            pe.sem_inc(gate_pe, 1)
            for k in range(KE):
                last = nc.tensor.transpose(ps[:, 1, k * SLOTS:(k + 1) * SLOTS], hd[:, u, k::KE],
                                           ident[0:SLOTS, 0:SLOTS])
            last.then_inc(S["hps"][u], 1)

        def down(pe, u, n, n_other):
            pe.wait_ge(S["wd"][u], 16 * n + 16)
            pe.wait_ge(S["hT"][u], n + 1)
            pe.wait_ge(S["yo"][1 - u], 2 * n_other)
            for b in range(2):
                for k in range(KE):
                    last = nc.tensor.matmul(ps[0:SLOTS, 6 + b], hT[:, u, k], wd[:, u, k, b * 512:(b + 1) * 512],
                                            start=k == 0, stop=k == KE - 1)
            last.then_inc(S["dn"][u], 1)

        def gate_act(act, u, n):
            act.wait_ge(S["gu"][u], n + 1)
            act.wait_ge(S["hd"][u], n)
            act.activation(sg[:, u], ps[0:SLOTS, 2 + u], ACT.Silu).then_inc(S["sg"][u], 1)

        def result_out(act, row, u, n):
            act.wait_ge(S["dn"][u], n + 1)
            act.wait_ge(S["ys"][u], 16 * n)
            for b in range(2):
                act.activation(yo[:, u, b * 512:(b + 1) * 512], ps[0:SLOTS, 6 + b], ACT.Copy).then_inc(S["yo"][u], 1)
            act.wait_ge(S["yo"][u], 2 * n + 2)
            act.dma_start(Y_rows[row], yo[:, u]).then_inc(S["ys"][u], 16)

        def tokens_out(dve, u, n):
            dve.wait_ge(S["xps"][u], n + 1)
            dve.wait_ge(S["gu"][u], n)
            dve.tensor_copy(xT[:, u], ps[:, 0, 0:KD * SLOTS].rearrange("p (k s) -> p k s", k=KD)).then_inc(S["xT"][u], 1)

        def hidden(dve, u, n):
            dve.wait_ge(S["sg"][u], n + 1)
            dve.wait_ge(S["hps"][u], n)
            dve.tensor_tensor(hd[:, u], ps[0:SLOTS, 4 + u], sg[:, u], ALU.mult).then_inc(S["hd"][u], 1)

        def hidden_out(dve, u, n):
            dve.wait_ge(S["hps"][u], n + 1)
            dve.wait_ge(S["dn"][u], n)
            dve.tensor_copy(hT[:, u], ps[:, 1, 0:KE * SLOTS].rearrange("p (k s) -> p k s", k=KE)).then_inc(S["hT"][u], 1)

        TURNS = N_EXPERTS // H
        with nc.Block() as block:
            @block.sync
            def _(sp):
                with sp.Fori(0, TURNS) as t:
                    for u in range(H):
                        sp.wait_ge(S["gu"][u], t)
                        expert_weights(sp, t * H + u, u)
                        sp.wait_ge(S["dn"][u], t)
                        down_weights(sp, t * H + u, u)

            @block.gpsimd
            def _(pool):
                pool.memset(zero[:], 0.0).then_inc(cleared, 1)
                pool.wait_ge(cleared, 1)
                for b in range(N_EXPERTS, MOE_BLOCKS):
                    pool.dma_start(Y_rows[b], zero[:]).then_inc(opened, 16)
                with pool.Fori(0, TURNS) as t:
                    for u in range(H):
                        gather(pool, slice_of(t * H + u), u, t)
                pool.wait_ge(opened, 16 * (SPILL + 1))

            @block.tensor
            def _(pe):
                turn_tokens(pe, 0, 0, 0)
                gate_up(pe, 0, 0)
                turn_tokens(pe, 1, 0, 1)
                with pe.Fori(0, TURNS - 1) as t:
                    gate_up(pe, 1, t)
                    turn_hidden(pe, 0, t, t)
                    turn_tokens(pe, 0, t + 1, t + 1)
                    down(pe, 0, t, t)
                    gate_up(pe, 0, t + 1)
                    turn_hidden(pe, 1, t, t + 1)
                    turn_tokens(pe, 1, t + 1, t + 2)
                    down(pe, 1, t, t + 1)
                gate_up(pe, 1, TURNS - 1)
                turn_hidden(pe, 0, TURNS - 1, TURNS - 1)
                down(pe, 0, TURNS - 1, TURNS - 1)
                turn_hidden(pe, 1, TURNS - 1, TURNS)
                down(pe, 1, TURNS - 1, TURNS)

            @block.vector
            def _(dve):
                tokens_out(dve, 0, 0)
                tokens_out(dve, 1, 0)
                hidden(dve, 0, 0)
                with dve.Fori(0, TURNS - 1) as t:
                    hidden_out(dve, 0, t)
                    tokens_out(dve, 0, t + 1)
                    hidden(dve, 1, t)
                    hidden_out(dve, 1, t)
                    tokens_out(dve, 1, t + 1)
                    hidden(dve, 0, t + 1)
                hidden_out(dve, 0, TURNS - 1)
                hidden(dve, 1, TURNS - 1)
                hidden_out(dve, 1, TURNS - 1)

            @block.scalar
            def _(act):
                gate_act(act, 0, 0)
                with act.Fori(0, TURNS - 1) as t:
                    gate_act(act, 1, t)
                    result_out(act, t * H, 0, t)
                    gate_act(act, 0, t + 1)
                    result_out(act, t * H + 1, 1, t)
                gate_act(act, 1, TURNS - 1)
                result_out(act, (TURNS - 1) * H, 0, TURNS - 1)
                result_out(act, (TURNS - 1) * H + 1, 1, TURNS - 1)
                for u in range(H):
                    act.wait_ge(S["ys"][u], 16 * TURNS)

        def spilled(engine, body):
            n_spill = engine.value_load(spill[0:1, SPILL + 1:SPILL + 2], min_val=0, max_val=SPILL + 1)
            with engine.Fori(0, SPILL + 1) as b:
                with engine.If(n_spill > b):
                    body(b)
            return n_spill

        with nc.Block() as block:
            @block.sync
            def _(sp):
                def body(b):
                    e = sp.value_load(spill[0:1, slice_of(b)], min_val=0, max_val=N_EXPERTS - 1)
                    sp.wait_ge(S["gu"][0], TURNS + b)
                    expert_weights(sp, e, 0)
                    sp.wait_ge(S["dn"][0], TURNS + b)
                    down_weights(sp, e, 0)
                spilled(sp, body)

            @block.gpsimd
            def _(pool):
                spilled(pool, lambda b: gather(pool, slice_of(b + N_EXPERTS), 0, b + TURNS))

            @block.tensor
            def _(pe):
                def body(b):
                    turn_tokens(pe, 0, TURNS + b, TURNS)
                    gate_up(pe, 0, TURNS + b)
                    turn_hidden(pe, 0, TURNS + b, TURNS)
                    down(pe, 0, TURNS + b, TURNS)
                spilled(pe, body)

            @block.vector
            def _(dve):
                def body(b):
                    tokens_out(dve, 0, TURNS + b)
                    hidden(dve, 0, TURNS + b)
                    hidden_out(dve, 0, TURNS + b)
                spilled(dve, body)

            @block.scalar
            def _(act):
                def body(b):
                    gate_act(act, 0, TURNS + b)
                    result_out(act, b + N_EXPERTS, 0, TURNS + b)
                n_spill = spilled(act, body)
                act.wait_ge(S["ys"][0], (n_spill + TURNS) * 16)
                act.sem_inc(gate_act_end, 1)


def slice_of(n):
    return bass.ds(n, 1)


def combine(core, Y_flat, slots_u, gates):
    nc, ps, ident = core.nc, core.psum, core.ident
    with core.stage("comb") as st:
        g = st.sb("g", [P, 2, NT, D])
        own = st.sem("own")
        got = [st.sem(f"got{n}") for n in range(2 * NT)]
        mixed, t_ps, t_out = st.sem("mixed"), st.sem("tps"), st.sem("tout")
        with nc.Block() as block:
            @block.gpsimd
            def _(pool):
                for i in range(NT):
                    for j in range(2):
                        pool.indirect_dma_start(
                            out=g[:, j, i], out_offset=None, in_=Y_flat,
                            in_offset=bass.IndirectOffsetOnAxis(ap=slots_u[:, j, i:i + 1], axis=0)
                        ).then_inc(got[2 * i + j], 16)

            @block.vector
            def _(dve):
                step = Chain(dve, own)
                for i in range(NT):
                    dve.wait_ge(got[2 * i], 16)
                    dve.wait_ge(got[2 * i + 1], 16)
                    step(dve.tensor_scalar(g[:, 1, i], g[:, 1, i], gates[:, 1, i:i + 1], None, ALU.mult))
                    dve.scalar_tensor_tensor(out=g[:, 0, i], in0=g[:, 0, i], scalar=gates[:, 0, i:i + 1],
                                             in1=g[:, 1, i], op0=ALU.mult, op1=ALU.add).then_inc(mixed, 1)
                for k in range(KD):
                    dve.wait_ge(t_ps, k + 1)
                    dve.tensor_tensor(core.h[:, k, MAIN], core.h[:, k, MAIN], ps[:, k], ALU.add).then_inc(t_out, 1)

            @block.tensor
            def _(pe):
                pe.wait_ge(mixed, NT)
                for k in range(KD):
                    for i in range(NT):
                        last = nc.tensor.transpose(ps[:, k, i * P:(i + 1) * P], g[:, 0, i, k * P:(k + 1) * P], ident[:])
                    last.then_inc(t_ps, 1)


def first_ffn(core, A):
    nc = core.nc
    T_rows = nc.dram_tensor("token_rows", (SEQ, D), F32, kind="Internal").ap()
    Y_rows = nc.dram_tensor("expert_rows", (MOE_BLOCKS, SLOTS, D), F32, kind="Internal").ap()
    slot_tok = nc.dram_tensor("slot_tokens", (MOE_BLOCKS * SLOTS, 1), U32, kind="Internal").ap()
    with core.stage("ffn1") as st:
        slots_u, gates = st.sb("slots", [P, 2, NT], U32), st.sb("gates", [P, 2, NT])
        block_tok, spill = st.sb("block_tok", [SLOTS, MOE_BLOCKS], U32), st.sb("spill", [1, SPILL + 2], U32)
        with core.stage("ffn1r") as s2:
            t = s2.sb("t", [P, KD, SEQ])
            norm(core, "n2", core.h[:, :, MAIN], t, core.vec[:, VEC["ffn"]], D)
            route(core, A, t, T_rows, slot_tok, slots_u, gates, block_tok, spill)
        experts(core, A, T_rows, Y_rows, block_tok, spill)
        combine(core, Y_rows.rearrange("b s d -> (b s) d"), slots_u, gates)


def hgrn(core, A, z, v, y):
    nc, ps, vec, ident = core.nc, core.psum, core.vec, core.ident
    NC = SEQ // CHUNK
    NL = len(LEVELS) + 1
    with core.stage("hg") as st:
        mask = st.sb("mask", [P, NL, P], U32)
        heads = st.sb("heads", [P, P])
        lb = st.sb("lb", [P, 4, KH])
        q, f = z[:, 0:KH], z[:, KH:2 * KH]
        k = f
        b, eb, qe, kd = (st.sb(n, [P, KH, SEQ]) for n in ("b", "eb", "qe", "kd"))
        F = st.sb("F", [P, 2, KH, SEQ])
        Q, K = st.sb("Q", [P, 2, KH, SEQ]), st.sb("K", [P, 2, KH, SEQ])
        kdt = Q[:, 1]
        reset = K[:, 1, 0]
        vz = st.sb("vz", [P, NT, HG_H, P])
        att = st.sb("att", [P, NT, 2, KH, P])
        state = st.sb("state", [P, KH, NC, P])
        (loaded, acts, dves, pools, lb_in, lb_out, sig, forget, logf, b_ready, e_ready, k_ready, q_ready, kt_ps,
         kt_out, u_ps, state_ready, cleared, d_ready, f_ready, ql, kl, s_ps, s_out, o_ps, sq_ready, ss_ps, inv_ready,
         rs_ready, silu_g) = (st.sem(n) for n in (
             "ld", "act", "dve", "pool", "lbi", "lbo", "sig", "fg", "lf", "b", "e", "k", "q", "ktp", "kto", "u",
             "st", "cl", "d", "f", "ql", "kl", "sp", "so", "o", "sq", "ss", "inv", "rs", "sg"))
        with nc.Block() as block:
            @block.sync
            def _(sp):
                for dst, src in ((reset, "reset_main"), (mask[:], "level_masks"), (heads[:], "head_pairs")):
                    sp.dma_start(dst, A[src]).then_inc(loaded, 16)

            @block.gpsimd
            def _(pool):
                step = Chain(pool, pools)
                step(pool.memset(vz[:], 0.0))
                step(pool.memset(state[:], 0.0))
                vv = v[:].rearrange("p i (h e) -> p i h e", h=HG_H)
                for half in range(2):
                    step(pool.tensor_copy(vz[:, :, half::2, half * HG_D:(half + 1) * HG_D], vv[:, :, half::2, :]))
                pool.sem_inc(cleared, 1)
                for n in range(NL - 1):
                    pool.wait_ge(f_ready, n + 1)
                    if n >= 2:
                        pool.wait_ge(s_ps, NT * (n - 1))
                    pool.tensor_tensor(K[:, n % 2], k, F[:, n % 2], ALU.mult).then_inc(kl, 1)

            @block.scalar
            def _(act):
                step = Chain(act, acts)
                act.activation(f, f, ACT.Sigmoid).then_inc(sig, 1)
                step(act.activation(q, q, ACT.Silu))
                act.activation(z[:, 2 * KH:3 * KH], z[:, 2 * KH:3 * KH], ACT.Silu).then_inc(silu_g, 1)
                act.sem_inc(q_ready, 1)
                act.wait_ge(lb_in, 1)
                act.activation(lb[:, 0:2], lb[:, 0:2], ACT.Exp).then_inc(lb_out, 1)
                act.wait_ge(forget, 1)
                act.activation(eb[:], kd[:], ACT.Ln).then_inc(logf, 1)
                act.wait_ge(b_ready, 1)
                step(act.activation(eb[:], b[:], ACT.Exp))
                act.activation(kd[:], kd[:], ACT.Exp).then_inc(e_ready, 1)
                for n in range(NL - 1):
                    act.wait_ge(d_ready, n + 1)
                    act.activation(F[:, n % 2], F[:, n % 2], ACT.Exp).then_inc(f_ready, 1)
                for p in range(KH):
                    act.wait_ge(o_ps, p + 1)
                    act.activation(Q[:, 0, p], ps[:, p], ACT.Square).then_inc(sq_ready, 1)
                for p in range(KH):
                    act.wait_ge(inv_ready, p + 1)
                    act.activation(F[:, 0, p], F[:, 1, p], ACT.Sqrt).then_inc(rs_ready, 1)

            @block.vector
            def _(dve):
                step = Chain(dve, dves)
                lo, hi = vec[:, VEC["lb0"]], vec[:, VEC["lb1"]]
                step(dve.tensor_tensor(lb[:, 2], lo, hi, ALU.max))
                step(dve.tensor_tensor(lb[:, 0], lo, lb[:, 2], ALU.subtract))
                step(dve.tensor_tensor(lb[:, 1], hi, lb[:, 2], ALU.subtract))
                dve.sem_inc(lb_in, 1)
                dve.wait_ge(lb_out, 1)
                step(dve.tensor_tensor(lb[:, 2], lb[:, 0], lb[:, 1], ALU.add))
                step(dve.reciprocal(lb[:, 3], lb[:, 2]))
                step(dve.tensor_tensor(lb[:, 0], lb[:, 0], lb[:, 3], ALU.mult))
                step(dve.tensor_scalar(lb[:, 1], lb[:, 0], -1.0, 1.0, ALU.mult, ALU.add))
                dve.wait_ge(sig, 1)
                for p in range(KH):
                    step(dve.tensor_scalar(kd[:, p], f[:, p], lb[:, 1, p:p + 1], lb[:, 0, p:p + 1], ALU.mult, ALU.add))
                dve.sem_inc(forget, 1)
                step(dve.tensor_scalar(k, kd[:], -1.0, 1.0, ALU.mult, ALU.add))
                dve.wait_ge(q_ready, 1)
                step(dve.tensor_scalar(q, q, float(HG_D) ** -0.5, None, ALU.mult))
                dve.wait_ge(loaded, 48)
                dve.wait_ge(logf, 1)
                for p in range(KH):
                    step(dve.tensor_tensor_scan(b[:, p], reset, eb[:, p], 0.0, ALU.mult, ALU.add))
                for p in range(KH):
                    bc = b[:, p].rearrange("p (n c) -> p n c", c=CHUNK)
                    step(dve.tensor_tensor(kd[:, p].rearrange("p (n c) -> p n c", c=CHUNK),
                                           bc[:, :, CHUNK - 1:CHUNK].to_broadcast([P, NC, CHUNK]), bc, ALU.subtract))
                dve.sem_inc(b_ready, 1)

                def exponents(n):
                    m = LEVELS[n]
                    if n >= 2:
                        dve.wait_ge(kl, n - 1)
                    fb = F[:, n % 2].rearrange("p t (n c) -> p (t n) c", c=2 * m)
                    bb = b[:].rearrange("p t (n c) -> p (t n) c", c=2 * m)
                    mid = bb[:, :, m - 1:m].to_broadcast([P, KH * SEQ // (2 * m), m])
                    step(dve.tensor_tensor(fb[:, :, m:], bb[:, :, m:], mid, ALU.subtract))
                    step(dve.tensor_tensor(fb[:, :, 0:m], mid, bb[:, :, 0:m], ALU.subtract))
                    dve.sem_inc(d_ready, 1)

                def queries(n):
                    dve.wait_ge(f_ready, n + 1)
                    if n >= 2:
                        dve.wait_ge(s_ps, NT * (n - 1))
                    step(dve.tensor_tensor(Q[:, n % 2], q, F[:, n % 2], ALU.mult))
                    dve.sem_inc(ql, 1)

                exponents(0)
                step(dve.memset(att[:], 0.0))
                dve.wait_ge(e_ready, 1)
                step(dve.tensor_tensor(qe[:], q, eb[:], ALU.mult))
                step(dve.tensor_tensor(kd[:], k, kd[:], ALU.mult))
                dve.sem_inc(k_ready, 1)
                exponents(1)
                queries(0)
                for i in range(NT):
                    dve.wait_ge(kt_ps, i + 1)
                    dve.tensor_copy(kdt[:, i], ps[:, i]).then_inc(kt_out, 1)
                dve.wait_ge(cleared, 1)
                for j in range(NC - 1):
                    dve.wait_ge(u_ps, j + 1)
                    for p in range(KH):
                        for half in range(2):
                            r = slice(64 * half, 64 * half + 64)
                            last = dve.scalar_tensor_tensor(
                                out=state[r, p, j + 1, r], in0=state[r, p, j, r],
                                scalar=eb[r, p, (j + 1) * CHUNK - 1:(j + 1) * CHUNK],
                                in1=ps[r, j, p * P + 64 * half:p * P + 64 * half + 64], op0=ALU.mult, op1=ALU.add)
                    step(last)
                dve.sem_inc(state_ready, 1)
                for n in range(NL):
                    if n < NL - 1:
                        if n + 2 < NL - 1:
                            exponents(n + 2)
                        if n + 1 < NL - 1:
                            queries(n + 1)
                    for i in range(NT):
                        s = n * NT + i
                        dve.wait_ge(s_ps, s + 1)
                        for half in range(2):
                            dve.copy_predicated(att[:, i, half],
                                                mask[:, n:n + 1].to_broadcast([P, KH, P]),
                                                ps[:, 2 * (s % 4) + half].rearrange("p (h c) -> p h c", c=P)
                                                ).then_inc(s_out, 1)
                for p in range(KH):
                    dve.wait_ge(ss_ps, p + 1)
                    step(dve.tensor_scalar(F[:, 0, p], ps[:, 4 + p], 1.0 / HG_D, EPS, ALU.mult, ALU.add))
                    dve.reciprocal(F[:, 1, p], F[:, 0, p]).then_inc(inv_ready, 1)
                dve.wait_ge(silu_g, 1)
                for p in range(KH):
                    dve.wait_ge(rs_ready, p + 1)
                    step(dve.scalar_tensor_tensor(out=y[:, p], in0=ps[:, p], scalar=vec[:, VEC["hg_out"]][:, p:p + 1],
                                                  in1=F[:, 0, p], op0=ALU.mult, op1=ALU.mult))
                    step(dve.tensor_tensor(y[:, p], y[:, p], z[:, 2 * KH + p], ALU.mult))

            @block.tensor
            def _(pe):
                pe.wait_ge(loaded, 48)
                pe.wait_ge(k_ready, 1)
                for i in range(NT):
                    for p in range(KH):
                        last = nc.tensor.transpose(ps[:, i, p * P:(p + 1) * P], kd[:, p, i * P:(i + 1) * P], ident[:])
                    last.then_inc(kt_ps, 1)
                for j in range(NC - 1):
                    i, r = j // 2, slice(CHUNK * (j % 2), CHUNK * (j % 2) + CHUNK)
                    pe.wait_ge(kt_out, NT)
                    for p in range(KH):
                        last = nc.tensor.matmul(ps[:, j, p * P:(p + 1) * P], kdt[r, i, p * P:(p + 1) * P],
                                                v[r, i, p * P:(p + 1) * P], start=True, stop=True)
                    last.then_inc(u_ps, 1)
                pe.wait_ge(state_ready, 1)
                for n in range(NL):
                    if n < NL - 1:
                        pe.wait_ge(ql, n + 1)
                        pe.wait_ge(kl, n + 1)
                    for i in range(NT):
                        s = n * NT + i
                        if s >= 4:
                            pe.wait_ge(s_out, 2 * (s - 3))
                        c = slice(P * i, P * (i + 1))
                        for h in range(HG_H):
                            r = slice(64 * (h % 2), 64 * (h % 2) + 64)
                            kk = K[r, n % 2, h // 2, c] if n < NL - 1 else k[r, h // 2, c]
                            qq = Q[r, n % 2, h // 2, c] if n < NL - 1 else z[r, h // 2, c]
                            last = nc.tensor.matmul(ps[:, 2 * (s % 4) + h % 2, (h // 2) * P:(h // 2 + 1) * P], kk, qq,
                                                    start=True, stop=True)
                        last.then_inc(s_ps, 1)
                pe.wait_ge(s_out, 2 * NL * NT)
                pe.wait_ge(cleared, 1)
                for p in range(KH):
                    for i in range(NT):
                        for half in range(2):
                            last = nc.tensor.matmul(ps[:, p, i * P:(i + 1) * P], vz[:, i, 2 * p + half], att[:, i, half, p],
                                                    start=half == 0, stop=False)
                        for j in (2 * i, 2 * i + 1):
                            last = nc.tensor.matmul(ps[:, p, j * CHUNK:(j + 1) * CHUNK], state[:, p, j],
                                                    qe[:, p, j * CHUNK:(j + 1) * CHUNK], start=False, stop=j % 2 == 1)
                    last.then_inc(o_ps, 1)
                for p in range(KH):
                    pe.wait_ge(sq_ready, p + 1)
                    nc.tensor.matmul(ps[:, 4 + p], heads[:], Q[:, 0, p], start=True, stop=True).then_inc(ss_ps, 1)


def convolve(core, z, y):
    nc, w = core.nc, core.vec[:, VEC["conv"]]
    with core.stage("conv") as st:
        own = st.sem("own")
        with nc.Block() as block:
            @block.scalar
            def _(act):
                act.activation(z[:, 3 * KH:], z[:, 3 * KH:], ACT.Sigmoid)

            @block.vector
            def _(dve):
                step = Chain(dve, own)
                u = z[:, KH:2 * KH]
                step(dve.tensor_tensor(u, u, z[:, 2 * KH:3 * KH], ALU.mult))
                for p in range(KH):
                    step(dve.tensor_scalar(y[:, p], u[:, p], w[:, 2 * KH + p:2 * KH + p + 1], None, ALU.mult))
                    for back in (1, 2):
                        tap = (2 - back) * KH + p
                        step(dve.scalar_tensor_tensor(out=y[:, p, back:], in0=u[:, p, 0:SEQ - back],
                                                      scalar=w[:, tap:tap + 1], in1=y[:, p, back:],
                                                      op0=ALU.mult, op1=ALU.add))
                step(dve.tensor_tensor(y[:], y[:], z[:, 0:KH], ALU.mult))


def second_mixer(core, A):
    with core.stage("mix2") as st:
        xn = st.sb("xn", [P, KD, SEQ])
        ya = st.sb("ya", [P, KH, SEQ])
        seq = (slice(0, SEQ),)
        norm(core, "n3", core.h[:, :, MAIN], core.h[:, :, MAIN], core.vec[:, VEC["final"]], D)
        norm(core, "n4", core.h[:, :, MAIN], xn, core.vec[:, VEC["mix2"]], D)
        with core.stage("mix2a") as s2:
            z, v = s2.sb("z", [P, 3 * KH, SEQ]), s2.sb("v", [P, NT, HG_W])
            project(core, "in2a", A["w_in2a"], xn, 3 * KH, seq,
                    lambda act, m, acc, c: act.activation(z[:, m], acc, ACT.Copy))
            by_token(core, "in2v", A["w_v2"], xn, v, [(i, P * i, P) for i in range(NT)])
            hgrn(core, A, z, v, ya)
        with core.stage("mix2b") as s2:
            z = s2.sb("z", [P, 28, SEQ])
            yb = s2.sb("yb", [P, KH, SEQ])
            project(core, "in2b", A["w_in2b"], xn, 28, seq,
                    lambda act, m, acc, c: act.activation(z[:, m], acc, ACT.Copy))
            convolve(core, z, yb)
            ga, gb = z[:, 12:20], z[:, 20:28]
            project(core, "bra", A["w_bra"], ya, KD, seq,
                    lambda dve, m, acc, c: dve.tensor_tensor(ga[:, m], ga[:, m], acc, ALU.mult), on_vector=True)
            project(core, "brb", A["w_brb"], yb, KD, seq,
                    lambda dve, m, acc, c: dve.tensor_tensor(gb[:, m], gb[:, m], acc, ALU.mult), on_vector=True)
            with core.nc.Block() as block:
                @block.vector
                def _(dve):
                    dve.tensor_tensor(ga, ga, gb, ALU.add)
            add_projection(core, "out2", A["w_out2"], ga)


def retrieve(core, A, q, which):
    nc, ps, ident = core.nc, core.psum, core.ident
    HS, H, K = 2 * PEER_H, PEER_H, TOPK
    LOW = -3.0e38
    with core.stage("top") as st:
        keys = st.sb("keys", [P, HS, NKEYS])
        io = st.sb("iota", [P, K])
        sc, sc2 = st.sb("sc", [P, 2, HS, NKEYS]), st.sb("sc2", [P, HS, NKEYS])
        val, idx = st.sb("val", [P, HS, K]), st.sb("idx", [P, HS, K], U32)
        idf = st.sb("idf", [P, HS, K])
        cand, cand2 = st.sb("cand", [P, H, K * K]), st.sb("cand2", [P, H, K * K])
        top, pos = st.sb("top", [P, H, K]), st.sb("pos", [P, H, K], U32)
        part, pf = st.sb("part", [P, 2, H, K], U32), st.sb("pf", [P, 2, H, K])
        hit = st.sb("hit", [P, H, K, K])
        found = st.sb("found", [P, 3, H, K])
        ex, sums = st.sb("ex", [P, H, K]), st.sb("sums", [P, 2, H])
        loaded, own, s_ps, s_out, free, e_in, e_out, res, t_ps, t_out = (
            st.sem(n) for n in ("ld", "own", "sp", "so", "fr", "ei", "eo", "res", "tp", "to"))
        with nc.Block() as block:
            @block.sync
            def _(sp):
                sp.dma_start(keys[:], A["keys"]).then_inc(loaded, 16)
                sp.dma_start(io[:], A["iota16"]).then_inc(loaded, 16)

            def turn(pe, i):
                pe.wait_ge(res, i + 1)
                if i >= 1:
                    pe.wait_ge(t_out, i)
                for n in range(3):
                    last = nc.tensor.transpose(ps[:, 4, n * P:(n + 1) * P], found[:, n].rearrange("p h k -> p (h k)"), ident[:])
                last.then_inc(t_ps, 1)

            @block.tensor
            def _(pe):
                pe.wait_ge(loaded, 32)
                for i in range(NT):
                    if i >= 1:
                        pe.wait_ge(s_out, i)
                    for n in range(HS):
                        last = nc.tensor.matmul(ps[:, n // 4, (n % 4) * P:(n % 4 + 1) * P], q[:, n, i * P:(i + 1) * P],
                                                keys[:, n], start=True, stop=True)
                    last.then_inc(s_ps, 1)
                    if i >= 1:
                        turn(pe, i - 1)
                turn(pe, NT - 1)

            @block.scalar
            def _(act):
                def scores_out(i):
                    act.wait_ge(s_ps, i + 1)
                    if i >= 2:
                        act.wait_ge(free, i - 1)
                    act.activation(sc[:, i % 2], ps[:, 0:4].rearrange("p b (n c) -> p (b n) c", c=P), ACT.Copy).then_inc(s_out, 1)

                scores_out(0)
                for i in range(NT):
                    if i + 1 < NT:
                        scores_out(i + 1)
                    act.wait_ge(e_in, i + 1)
                    act.activation(ex[:], ex[:], ACT.Exp).then_inc(e_out, 1)
                    act.wait_ge(t_ps, i + 1)
                    act.activation(which[:, :, i * P:(i + 1) * P],
                                   ps[:, 4, 0:3 * P].rearrange("p (n c) -> p n c", c=P), ACT.Copy).then_inc(t_out, 1)

            @block.vector
            def _(dve):
                step = Chain(dve, own)
                dve.wait_ge(loaded, 32)

                def best(values, places, src, spare):
                    step(dve.max(values[:, 0:8], src))
                    dve.max_index(places[:, 0:8], values[:, 0:8], src)
                    step(dve.match_replace(out=spare, in_to_replace=values[:, 0:8], in_values=src, imm_value=LOW))
                    step(dve.max(values[:, 8:16], spare))
                    step(dve.max_index(places[:, 8:16], values[:, 8:16], spare))

                for i in range(NT):
                    dve.wait_ge(s_out, i + 1)
                    for n in range(HS):
                        best(val[:, n], idx[:, n], sc[:, i % 2, n], sc2[:, n])
                    dve.sem_inc(free, 1)
                    pair = val[:].rearrange("p (h s) k -> p h s k", s=2)
                    for h in range(H):
                        step(dve.tensor_tensor(cand[:, h].rearrange("p (a b) -> p a b", b=K),
                                               pair[:, h, 0].unsqueeze(2).to_broadcast([P, K, K]),
                                               pair[:, h, 1].unsqueeze(1).to_broadcast([P, K, K]), ALU.add))
                    for h in range(H):
                        best(top[:, h], pos[:, h], cand[:, h], cand2[:, h])
                    step(dve.tensor_tensor(ex[:], top[:], top[:, :, 0:1].to_broadcast([P, H, K]), ALU.subtract))
                    dve.sem_inc(e_in, 1)
                    step(dve.tensor_copy(idf[:], idx[:]))
                    step(dve.tensor_scalar(part[:, 0], pos[:], 4, None, ALU.logical_shift_right))
                    step(dve.tensor_scalar(part[:, 1], pos[:], K - 1, None, ALU.bitwise_and))
                    step(dve.tensor_copy(pf[:], part[:]))
                    if i >= 1:
                        dve.wait_ge(t_ps, i)
                    of = idf[:].rearrange("p (h s) k -> p h s k", s=2)
                    for s in range(2):
                        step(dve.tensor_tensor(hit[:], pf[:, s].unsqueeze(3).to_broadcast([P, H, K, K]),
                                               io[:].unsqueeze(1).unsqueeze(1).to_broadcast([P, H, K, K]), ALU.is_equal))
                        step(dve.tensor_tensor(hit[:], hit[:], of[:, :, s].unsqueeze(2).to_broadcast([P, H, K, K]), ALU.mult))
                        step(dve.tensor_reduce(found[:, s], hit[:], AX.X, ALU.add))
                    dve.wait_ge(e_out, i + 1)
                    step(dve.tensor_reduce(sums[:, 0], ex[:], AX.X, ALU.add))
                    step(dve.reciprocal(sums[:, 1], sums[:, 0]))
                    step(dve.tensor_tensor(found[:, 2], ex[:], sums[:, 1].unsqueeze(2).to_broadcast([P, H, K]), ALU.mult))
                    dve.sem_inc(res, 1)


def spread_gates(core, A, which, G):
    nc, ps = core.nc, core.psum
    TB, HALF = 64, 8
    ROUNDS = TB // (2 * HALF)
    STORES = SEQ // TB
    with core.stage("spread") as st:
        io = st.sb("iota", [P, NKEYS])
        one, two = st.sb("one", [P, 2, HALF, NKEYS]), st.sb("two", [P, 2, HALF, NKEYS])
        cols = st.sb("cols", [P, 2, HALF])
        gs = st.sb("gs", [P, 2, NKEYS, TB])
        loaded, carried = st.sem("ld"), st.sem("carried")
        made1, made2, prod, copied, colsem = ([st.sem(f"{n}{u}") for u in range(2)] for n in ("m1", "m2", "pr", "cp", "co"))
        stored = [st.sem(f"sd{u}") for u in range(2)]

        def rounds(engine, body, after=None):
            with engine.Fori(0, STORES // 2) as o:
                for b in range(2):
                    with engine.Fori(0, ROUNDS) as r:
                        for u in range(2):
                            body(o, b, r, u, (o * 2 + b) * ROUNDS + r)
                    if after:
                        after(o, b)

        with nc.Block() as block:
            @block.sync
            def _(sp):
                sp.dma_start(io[:], A["iota128"]).then_inc(loaded, 16)
                with sp.Fori(0, STORES // 2) as o:
                    for b in range(2):
                        for u in range(2):
                            sp.wait_ge(copied[u], (o * 2 + b + 1) * (2 * ROUNDS))
                        sp.dma_start(G[:, :, bass.ds(o * 2 + b, 1)].rearrange("g n t x -> n (t g) x"),
                                     gs[:, b].rearrange("p (g k) t -> p g (k t)", k=GROUP)).then_inc(stored[b], 16)
                for b in range(2):
                    sp.wait_ge(stored[b], 16 * (STORES // 2))

            @block.vector
            def _(dve):
                dve.wait_ge(loaded, 16)

                def body(o, b, r, u, n):
                    dve.wait_ge(prod[u], n)
                    for x in range(HALF):
                        t = n * (2 * HALF) + (u * HALF + x)
                        last = dve.tensor_scalar(one[:, u, x], io[:], which[:, 0, bass.ds(t, 1)],
                                                 which[:, 2, bass.ds(t, 1)], ALU.is_equal, ALU.mult)
                    last.then_inc(made1[u], 1)
                rounds(dve, body)

            @block.gpsimd
            def _(pool):
                pool.wait_ge(loaded, 16)

                def body(o, b, r, u, n):
                    pool.wait_ge(made2[u], n)
                    pool.wait_ge(prod[u], n)
                    pool.tensor_copy(cols[:, u], which[:, 1, bass.ds(n * (2 * HALF) + u * HALF, HALF)]).then_inc(colsem[u], 1)
                    pool.wait_ge(colsem[u], n + 1)
                    pool.sem_inc(carried, 1)
                    for x in range(HALF):
                        last = pool.tensor_scalar(two[:, u, x], io[:], cols[:, u, x:x + 1], None, ALU.is_equal)
                    last.then_inc(made2[u], 1)
                rounds(pool, body)

            @block.tensor
            def _(pe):
                def body(o, b, r, u, n):
                    pe.wait_ge(made1[u], n + 1)
                    pe.wait_ge(made2[u], n + 1)
                    pe.wait_ge(copied[u], n * 2)
                    for x in range(HALF):
                        last = nc.tensor.matmul(ps[:, 2 * u + x // 4, (x % 4) * P:(x % 4 + 1) * P], two[:, u, x], one[:, u, x],
                                                start=True, stop=True)
                    last.then_inc(prod[u], 1)
                rounds(pe, body)

            @block.scalar
            def _(act):
                def body(o, b, r, u, n):
                    act.wait_ge(prod[u], n + 1)
                    act.wait_ge(stored[b], o * 16)
                    for c in range(2):
                        act.activation(gs[:, b, :, bass.ds(r * (2 * HALF) + (u * HALF + 4 * c), 4)],
                                       ps[:, 2 * u + c].rearrange("p (t n) -> p n t", n=NKEYS), ACT.Copy).then_inc(copied[u], 1)
                rounds(act, body)


def peer(core, A, hn, G):
    nc, ps = core.nc, core.psum
    SLOTS_U, TB = 4, 64
    TURNS = N_PASS // 2
    with core.stage("dense") as st:
        ub = st.sb("u", [P, SLOTS_U, KD, P])
        vb = st.sb("v", [P, 2, GROUP, D])
        gb = st.sb("g", [P, 2, SEQ // TB, GROUP, TB])
        ab = st.sb("a", [P, 2, GROUP, SEQ])
        u_ready = [st.sem(f"ur{n}") for n in range(SLOTS_U)]
        summed = [st.sem(f"su{n}") for n in range(SLOTS_U)]
        gelus = [st.sem(f"ge{n}") for n in range(SLOTS_U)]
        v_ready, g_ready, gated, outs = ([st.sem(f"{n}{b}") for b in range(2)] for n in ("vr", "gr", "ga", "ou"))
        added = [st.sem(f"ad{n}") for n in range(4)]

        def u_products(pe, t, b):
            for j in range(GROUP):
                n = t * 4 + (2 * b + j // SLOTS_U)
                s = j % SLOTS_U
                pe.wait_ge(u_ready[s], n * 16 + 16)
                pe.wait_ge(gelus[s], n)
                for k in range(KD):
                    last = nc.tensor.matmul(ps[:, s], ub[:, s, k], hn[:, k], start=k == 0, stop=k == KD - 1)
                last.then_inc(summed[s], 1)

        def v_products(pe, t, b):
            pe.wait_ge(v_ready[b], t * 16 + 16)
            pe.wait_ge(gated[b], t * GROUP + GROUP)
            for m in range(KD):
                pe.wait_ge(added[m % 4], t * 4 + (2 * b + m // 4))
                for j in range(GROUP):
                    last = nc.tensor.matmul(ps[:, 4 + m % 4], vb[:, b, j, m * P:(m + 1) * P], ab[:, b, j],
                                            start=j == 0, stop=j == GROUP - 1)
                last.then_inc(outs[b], 1)

        def gelu(act, t, b):
            act.wait_ge(outs[b], t * KD)
            for j in range(GROUP):
                n = t * 4 + (2 * b + j // SLOTS_U)
                act.wait_ge(summed[j % SLOTS_U], n + 1)
                act.activation(ab[:, b, j], ps[:, j % SLOTS_U], ACT.Gelu).then_inc(gelus[j % SLOTS_U], 1)

        def gate(dve, t, b):
            dve.wait_ge(g_ready[b], t * 16 + 16)
            for j in range(GROUP):
                n = t * 4 + (2 * b + j // SLOTS_U)
                dve.wait_ge(gelus[j % SLOTS_U], n + 1)
                a = ab[:, b, j].rearrange("p (s t) -> p s t", t=TB)
                dve.tensor_tensor(a, a, gb[:, b, :, j], ALU.mult).then_inc(gated[b], 1)

        def add(dve, t, b):
            for m in range(KD):
                dve.wait_ge(outs[b], t * KD + (m + 1))
                dve.tensor_tensor(core.h[:, m, MAIN], core.h[:, m, MAIN], ps[:, 4 + m % 4], ALU.add).then_inc(added[m % 4], 1)

        with nc.Block() as block:
            @block.sync
            def _(sp):
                with sp.Fori(0, TURNS) as t:
                    for b in range(2):
                        for j in range(GROUP):
                            s = j % SLOTS_U
                            sp.wait_ge(summed[s], t * 4 + (2 * b + j // SLOTS_U))
                            sp.dma_start(ub[:, s], A["peer_u"][(t * 2 + b) * GROUP + j]).then_inc(u_ready[s], 16)

            @block.gpsimd
            def _(pool):
                with pool.Fori(0, TURNS) as t:
                    for b in range(2):
                        pool.wait_ge(gated[b], t * GROUP)
                        pool.dma_start(gb[:, b], G[t * 2 + b].rearrange("n t (k x) -> n t k x", x=TB)
                                       ).then_inc(g_ready[b], 16)
                        pool.wait_ge(outs[b], t * KD)
                        pool.dma_start(vb[:, b], A["peer_v"][t * 2 + b]).then_inc(v_ready[b], 16)

            @block.tensor
            def _(pe):
                u_products(pe, 0, 0)
                with pe.Fori(0, TURNS - 1) as t:
                    u_products(pe, t, 1)
                    v_products(pe, t, 0)
                    u_products(pe, t + 1, 0)
                    v_products(pe, t, 1)
                u_products(pe, TURNS - 1, 1)
                v_products(pe, TURNS - 1, 0)
                v_products(pe, TURNS - 1, 1)

            @block.scalar
            def _(act):
                with act.Fori(0, TURNS) as t:
                    for b in range(2):
                        gelu(act, t, b)

            @block.vector
            def _(dve):
                gate(dve, 0, 0)
                with dve.Fori(0, TURNS - 1) as t:
                    gate(dve, t, 1)
                    add(dve, t, 0)
                    gate(dve, t + 1, 0)
                    add(dve, t, 1)
                gate(dve, TURNS - 1, 1)
                add(dve, TURNS - 1, 0)
                add(dve, TURNS - 1, 1)


def second_ffn(core, A, out):
    nc = core.nc
    G = nc.dram_tensor("gate_rows", (N_PASS, NKEYS, SEQ // 64, GROUP * 64), F32, kind="Internal").ap()
    with core.stage("ffn2") as st:
        hn = st.sb("hn", [P, KD, SEQ])
        norm(core, "n5", core.h[:, :, MAIN], hn, core.vec[:, VEC["ffn2"]], D)
        with core.stage("ffn2w") as s2:
            which = s2.sb("which", [P, 3, SEQ])
            with core.stage("ffn2q") as s3:
                q = s3.sb("q", [P, 2 * PEER_H, SEQ])
                project(core, "query", A["w_query"], hn, 2 * PEER_H, (slice(0, SEQ),),
                        lambda act, m, acc, c: act.activation(q[:, m], acc, ACT.Copy))
                retrieve(core, A, q, which)
            spread_gates(core, A, which, G)
        peer(core, A, hn, G)
        norm(core, "n6", core.h[:, :, MAIN], hn, core.vec[:, VEC["final2"]], D)
        saved = st.sem("saved")
        with nc.Block() as block:
            @block.sync
            def _(sp):
                sp.dma_start(out, hn[:]).then_inc(saved, 16)
                sp.wait_ge(saved, 16)


def program(nc, A, out):
    with ExitStack() as stack:
        core = Core(nc, stack)
        setup(core, A)
        first_mixer(core, A)
        first_ffn(core, A)
        core.recycle()
        second_mixer(core, A)
        core.recycle()
        second_ffn(core, A, out)


def _tiles(w):
    k, m = w.shape
    return w.reshape(k // P, P, m // P, P).transpose(2, 1, 0, 3)


def _rows(w):
    return w.reshape(w.shape[0] // P, P, w.shape[1]).transpose(1, 0, 2)


def _cols(g):
    return g.reshape(-1, P).T


def constants():
    c = {}
    s, t = np.arange(P)[:, None], np.arange(P)[None, :]
    c["ident"] = np.eye(P, dtype=np.float32)
    c["chunk_causal"] = ((s <= t) & (s // CHUNK == t // CHUNK)).astype(np.float32)
    starts = np.ones(L, np.float32)
    starts[0] = 0
    starts[META::CHUNK] = 0
    c["reset"] = np.broadcast_to(starts, (P, L))
    inv = (np.float32(10000.0) ** (-np.arange(0, ROPE, 2, dtype=np.float32) / np.float32(ROPE))).astype(np.float32)
    ang = (np.arange(L, dtype=np.float32)[:, None] * inv[None, :]).astype(np.float32)
    c["rope_cos"] = np.tile(np.cos(ang).T, (4, 1)).astype(np.float32)
    c["rope_sin"] = np.tile(np.sin(ang).T, (4, 1)).astype(np.float32)
    rot = np.zeros((P, P), np.float32)
    half = ROPE // 2
    for b in range(0, P, ROPE):
        for d in range(half):
            rot[b + half + d, b + d] = -1.0
            rot[b + d, b + half + d] = 1.0
    c["rope_rot"] = rot
    c["reset_main"] = np.broadcast_to(starts[MAIN], (P, SEQ))
    masks = [(s // (2 * m) == t // (2 * m)) & (s % (2 * m) < m) & (t % (2 * m) >= m) for m in LEVELS] + [s == t]
    c["level_masks"] = np.stack(masks, axis=1).astype(np.uint32)
    c["head_pairs"] = (s // HG_D == t // HG_D).astype(np.float32)
    c["iota16"] = np.broadcast_to(np.arange(TOPK, dtype=np.float32), (P, TOPK))
    c["iota128"] = np.broadcast_to(np.arange(NKEYS, dtype=np.float32), (P, NKEYS))
    c["before"] = (s < t).astype(np.float32)
    c["iota"] = np.broadcast_to(np.arange(N_EXPERTS, dtype=np.float32), (P, N_EXPERTS))
    c["tokens"] = np.arange(SEQ, dtype=np.uint32).reshape(NT, P).T
    return c


def lay_out(i):
    a = dict(constants())
    h = np.concatenate([i["meta_tokens"], i["x"][0]], axis=0)
    a["xT"] = h.T.reshape(KD, P, L).transpose(1, 0, 2)
    w = i["w_in"][0]
    kr = w[:, 1936:2000]
    a["w_in"] = _tiles(np.concatenate([w[:, 0:512], w[:, 1024:1536], w[:, 1552:1936], kr, kr], axis=1))
    a["w_v"] = _rows(w[:, 512:1024])
    a["w_alow"] = _rows(w[:, 1536:1552])
    a["w_a2"] = i["gla_w_a2"][0]
    qb = i["mla_w_qb"][0].reshape(2 * P, MLA_H, NOPE + ROPE)
    qb = np.concatenate([qb[:, :, :NOPE].reshape(2 * P, -1), qb[:, :, NOPE:].reshape(2 * P, -1)], axis=1)
    a["w_qb"] = qb.reshape(2, P, 6, P).transpose(1, 0, 2, 3)
    kvb = i["mla_w_kvb"][0].reshape(P, MLA_H, 2, P)
    a["w_kvb"] = kvb.transpose(0, 2, 1, 3).reshape(P, 2, 4 * P)
    a["w_out"] = _tiles(i["w_out"][0])
    a["w_router"] = _rows(np.concatenate([i["router_group_w"][0], i["router_expert_w"][0]], axis=1))
    a["b_router"] = np.broadcast_to(np.concatenate([i["router_group_b"][0], i["router_expert_b"][0]]),
                                    (P, N_GROUPS + N_EXPERTS))
    a["w_gate"] = i["expert_w_gate"][0].reshape(N_EXPERTS, P, KD, D_EXPERT)
    a["w_up"] = i["expert_w_up"][0].reshape(N_EXPERTS, P, KD, D_EXPERT)
    a["w_down"] = i["expert_w_down"][0].reshape(N_EXPERTS, P, KE, D)
    w = i["w_in_2"][0]
    a["w_in2a"] = _tiles(np.concatenate([w[:, 0:1024], w[:, 1536:2048]], axis=1))
    a["w_v2"] = _rows(w[:, 1024:1536])
    a["w_in2b"] = _tiles(w[:, 2048:])
    a["w_bra"] = _tiles(i["w_branch_hg_2"][0])
    a["w_brb"] = _tiles(i["w_branch_conv_2"][0])
    a["w_out2"] = _tiles(i["w_out_2"][0])
    a["w_query"] = _tiles(i["peer_w_query_2"][0])
    keys = np.stack([i["peer_keys1_2"][0], i["peer_keys2_2"][0]], axis=1)
    a["keys"] = keys.transpose(3, 0, 1, 2).reshape(P, 2 * PEER_H, NKEYS)
    a["peer_u"] = i["peer_u_2"][0].reshape(NKEYS, P, KD, P).transpose(0, 3, 2, 1)
    a["peer_v"] = i["peer_v_2"][0].reshape(N_PASS, GROUP, P, D).transpose(0, 2, 1, 3)
    vecs = {"mix": i["mix_norm"][0], "ffn": i["ffn_norm"][0], "final": i["final_norm"],
            "mix2": i["norm_mix_g_2"][0], "ffn2": i["norm_ffn_g_2"][0], "final2": i["norm_final_g_2"],
            "qn": i["mla_q_norm"][0], "kvn": i["mla_kv_norm"][0], "gla_out": i["gla_out_norm"][0],
            "b_a": i["gla_b_a"][0], "hg_out": i["hg_out_norm_g_2"][0],
            "lb0": i["hg_lb_logits_2"][0], "lb1": i["hg_lb_logits_2"][1], "conv": i["conv_w_2"][0].reshape(-1)}
    a["vectors"] = np.concatenate([_cols(vecs[n]) for n in VEC], axis=1)
    return a


def kernel(**inputs):
    import concourse.bacc as _bacc
    from concourse.bass_utils import run_bass_kernel_spmd as _run

    nc = _bacc.Bacc("TRN2", target_bir_lowering=False, num_devices=1)
    laid = lay_out({k: np.asarray(v) for k, v in inputs.items()})
    arrays, args = {}, {}
    for name, a in laid.items():
        a = np.ascontiguousarray(a)
        arrays[f"in_{name}"] = a
        args[name] = nc.dram_tensor(f"in_{name}", a.shape, mybir.dt.from_np(a.dtype), kind="ExternalInput").ap()
    out = nc.dram_tensor("out_dram", (P, KD, SEQ), F32, kind="ExternalOutput").ap()
    program(nc, args, out)
    r = _run(nc, [arrays], core_ids=[0])
    got = r.results[0]["out_dram"]
    return np.ascontiguousarray(np.asarray(got).transpose(2, 1, 0).reshape(1, SEQ, D))
```
